# Optimizing a Trainium2 kernel written in Bass

```python
import jax, jax.numpy as jnp
from jax import lax
import numpy as np

D_MODEL = 1024
BATCH = 1
SEQ = 512
DEPTH = 1
DEC_BATCH = 8
DEC_SEQ = 4
PAST_LEN = 4096
PAGE_SIZE = 128

HG_HEADS = 8
HG_DK = 128
HG_DV = 128
HG_WIDTH = HG_HEADS * HG_DK
HG_CHUNK = 64
SC_WIDTH = 1024
CONV_W = 3
N_GROUPS = 4
EXPERTS_PER_GROUP = 8
N_EXPERTS = N_GROUPS * EXPERTS_PER_GROUP
TOP_K = 2
D_EXPERT = 256
PLE_DIM = 256
EPS = 1e-6
IN_SIZES = (HG_WIDTH, HG_WIDTH, HG_WIDTH, HG_WIDTH, SC_WIDTH, SC_WIDTH, SC_WIDTH, D_MODEL, D_MODEL)
IN_COLS = 4 * HG_WIDTH + 3 * SC_WIDTH + 2 * D_MODEL

kernel_name = 'hgrn2_shortconv_hiermoe_ple_decode_step'

def rmsnorm(x, g):
    xf = x.astype(jnp.float32)
    r = lax.rsqrt(jnp.mean(xf * xf, axis=-1, keepdims=True) + EPS)
    return (xf * r).astype(x.dtype) * g

def hgrn_lower_bounds(lb_param):
    s = jax.nn.softmax(lb_param.astype(jnp.float32), axis=0)
    c = jnp.cumsum(s, axis=0)
    return c - c[0:1]

def hgrn2_scan(q, k, v, logf, s0):
    b, l = q.shape[0], q.shape[1]
    c = HG_CHUNK if l % HG_CHUNK == 0 else l
    n = l // c

    def to_chunks(t):
        return t.reshape(b, n, c, HG_HEADS, t.shape[-1]).transpose(1, 0, 3, 2, 4)

    qc, kc, vc, gc = to_chunks(q), to_chunks(k), to_chunks(v), to_chunks(logf)
    causal = jnp.tril(jnp.ones((c, c), dtype=bool))

    def step(s, inp):
        qi, ki, vi, gi = inp
        cum = jnp.cumsum(gi, axis=2)
        diff = cum[:, :, :, None, :] - cum[:, :, None, :, :]
        decay = jnp.exp(jnp.where(causal[:, :, None], diff, -jnp.inf))
        attn = jnp.sum(qi[:, :, :, None, :] * ki[:, :, None, :, :] * decay, axis=-1)
        o = (jnp.einsum('bhts,bhsv->bhtv', attn, vi)
             + jnp.einsum('bhtd,bhdv->bhtv', qi * jnp.exp(cum), s))
        last = cum[:, :, -1:, :]
        s_new = (jnp.exp(last[:, :, 0, :])[..., None] * s
                 + jnp.einsum('bhsd,bhsv->bhdv', ki * jnp.exp(last - cum), vi))
        return s_new, o

    s_fin, o = lax.scan(step, s0, (qc, kc, vc, gc))
    o = o.transpose(1, 0, 3, 2, 4).reshape(b, l, HG_HEADS, HG_DV)
    return o, s_fin

def hier_moe(h, w_rg, b_rg, w_re, b_re, w_gate, w_up, w_down):
    f32 = jnp.float32
    shp = h.shape
    t = h.reshape(-1, D_MODEL)
    n = t.shape[0]
    g_logits = (t @ w_rg).astype(f32) + b_rg.astype(f32)
    g_prob = jax.nn.softmax(g_logits, axis=-1)
    g_idx = jnp.argmax(g_logits, axis=-1)
    g_w = jnp.take_along_axis(g_prob, g_idx[:, None], axis=-1)
    e_logits = ((t @ w_re).astype(f32) + b_re.astype(f32)).reshape(n, N_GROUPS, EXPERTS_PER_GROUP)
    e_logits = jnp.take_along_axis(e_logits, g_idx[:, None, None], axis=1)[:, 0]
    e_prob = jax.nn.softmax(e_logits, axis=-1)
    top_p, top_i = lax.top_k(e_prob, TOP_K)
    top_p = top_p / jnp.sum(top_p, axis=-1, keepdims=True) * g_w
    within = jnp.sum(jax.nn.one_hot(top_i, EXPERTS_PER_GROUP, dtype=f32) * top_p[..., None], axis=1)
    combine = (jax.nn.one_hot(g_idx, N_GROUPS, dtype=f32)[:, :, None] * within[:, None, :])
    combine = combine.reshape(n, N_EXPERTS).astype(h.dtype)
    hid = jax.nn.silu(jnp.einsum('td,edf->tef', t, w_gate)) * jnp.einsum('td,edf->tef', t, w_up)
    out = jnp.einsum('tef,te,efd->td', hid, combine, w_down)
    return out.reshape(shp)

def trunk_layer(x, p, s_hg, conv_buf, lb, g_mix, w_in, g_hg_out, w_br_a, w_conv, w_br_b, w_out,
                g_ffn, w_rg, b_rg, w_re, b_re, w_gate, w_up, w_down, g_ple, w_ple_gate, w_ple_proj):
    f32 = jnp.float32
    bsz, l = x.shape[0], x.shape[1]
    h = rmsnorm(x, g_mix)
    proj = h @ w_in
    offs = np.cumsum(IN_SIZES)[:-1].tolist()
    q, fg, inp, og, cb, cc, ch, ga, gb = jnp.split(proj, offs, axis=-1)

    def heads(t):
        return t.reshape(bsz, l, HG_HEADS, -1).astype(f32)
    lbh = lb.reshape(HG_HEADS, HG_DK).astype(f32)
    fp = heads(fg)
    logf = jnp.logaddexp(jnp.log(lbh), jnp.log1p(-lbh) + jax.nn.log_sigmoid(fp))
    kf = (1.0 - lbh) * jax.nn.sigmoid(-fp)
    o, s_new = hgrn2_scan(jax.nn.silu(heads(q)), kf, heads(inp), logf, s_hg.astype(f32))
    o = rmsnorm(o, g_hg_out.reshape(HG_HEADS, HG_DV).astype(f32)).reshape(bsz, l, HG_WIDTH)
    o = (o * jax.nn.silu(og.astype(f32))).astype(x.dtype)
    y_a = o @ w_br_a

    u = cc * ch
    ext = jnp.concatenate([conv_buf.astype(u.dtype), u], axis=1)
    conv = sum(ext[:, j:j + l] * w_conv[j] for j in range(CONV_W))
    y_b = (cb * conv) @ w_br_b
    new_buf = ext[:, l:]

    x = x + (jax.nn.sigmoid(ga) * y_a + jax.nn.sigmoid(gb) * y_b) @ w_out

    x = x + hier_moe(rmsnorm(x, g_ffn), w_rg, b_rg, w_re, b_re, w_gate, w_up, w_down)

    x = x + jax.nn.sigmoid(rmsnorm(x, g_ple) @ w_ple_gate) * (p @ w_ple_proj)
    return x, s_new.astype(s_hg.dtype), new_buf

def run_trunk(x, p, s_hg, conv_buf, lbs, layer_params, g_final):
    hs, cs = [], []
    for li in range(DEPTH):
        x, s, c = trunk_layer(x, p[li], s_hg[li], conv_buf[li], lbs[li], *[w[li] for w in layer_params])
        hs.append(s)
        cs.append(c)
    return rmsnorm(x, g_final), jnp.stack(hs), jnp.stack(cs)

def setup_inputs(seed: int = 0) -> dict:
    key = jax.random.key(seed)
    ks = jax.random.split(key, 32)
    nrm = lambda k, shape, s=1.0: jax.random.normal(k, shape, jnp.float32) * s
    gain = lambda k, shape: 1.0 + 0.01 * jax.random.normal(k, shape, jnp.float32)
    return {
        'x_prompt': nrm(ks[0], (BATCH, SEQ, D_MODEL)),
        'x_sample': nrm(ks[1], (DEC_BATCH, DEC_SEQ, D_MODEL)),
        'state_hgrn': nrm(ks[2], (DEPTH, DEC_BATCH, HG_HEADS, HG_DK, HG_DV), 0.5),
        'state_conv': nrm(ks[3], (DEPTH, DEC_BATCH, CONV_W - 1, SC_WIDTH)),
        'p_prompt': nrm(ks[4], (DEPTH, BATCH, SEQ, PLE_DIM)),
        'p_sample': nrm(ks[5], (DEPTH, DEC_BATCH, DEC_SEQ, PLE_DIM)),
        'g_mix': gain(ks[6], (DEPTH, D_MODEL)),
        'w_in': nrm(ks[7], (DEPTH, D_MODEL, IN_COLS), D_MODEL ** -0.5),
        'hg_lower': nrm(ks[8], (DEPTH, HG_WIDTH)),
        'g_hg_out': gain(ks[9], (DEPTH, HG_WIDTH)),
        'w_br_a': nrm(ks[10], (DEPTH, HG_WIDTH, D_MODEL), HG_WIDTH ** -0.5),
        'w_conv': nrm(ks[11], (DEPTH, CONV_W, SC_WIDTH), CONV_W ** -0.5),
        'w_br_b': nrm(ks[12], (DEPTH, SC_WIDTH, D_MODEL), SC_WIDTH ** -0.5),
        'w_out': nrm(ks[13], (DEPTH, D_MODEL, D_MODEL), D_MODEL ** -0.5),
        'g_ffn': gain(ks[14], (DEPTH, D_MODEL)),
        'w_router_group': nrm(ks[15], (DEPTH, D_MODEL, N_GROUPS), D_MODEL ** -0.5),
        'b_router_group': nrm(ks[16], (DEPTH, N_GROUPS), 0.01),
        'w_router_expert': nrm(ks[17], (DEPTH, D_MODEL, N_EXPERTS), D_MODEL ** -0.5),
        'b_router_expert': nrm(ks[18], (DEPTH, N_EXPERTS), 0.01),
        'w_gate': nrm(ks[19], (DEPTH, N_EXPERTS, D_MODEL, D_EXPERT), D_MODEL ** -0.5),
        'w_up': nrm(ks[20], (DEPTH, N_EXPERTS, D_MODEL, D_EXPERT), D_MODEL ** -0.5),
        'w_down': nrm(ks[21], (DEPTH, N_EXPERTS, D_EXPERT, D_MODEL), D_EXPERT ** -0.5),
        'g_ple': gain(ks[22], (DEPTH, D_MODEL)),
        'w_ple_gate': nrm(ks[23], (DEPTH, D_MODEL, D_MODEL), D_MODEL ** -0.5),
        'w_ple_proj': nrm(ks[24], (DEPTH, PLE_DIM, D_MODEL), PLE_DIM ** -0.5),
        'g_final': gain(ks[25], (D_MODEL,)),
    }

def reference(x_prompt, x_sample, state_hgrn, state_conv, p_prompt, p_sample, g_mix, w_in, hg_lower,
              g_hg_out, w_br_a, w_conv, w_br_b, w_out, g_ffn, w_router_group, b_router_group,
              w_router_expert, b_router_expert, w_gate, w_up, w_down, g_ple, w_ple_gate, w_ple_proj,
              g_final):
    lbs = hgrn_lower_bounds(hg_lower)
    layer_params = (g_mix, w_in, g_hg_out, w_br_a, w_conv, w_br_b, w_out, g_ffn, w_router_group,
                    b_router_group, w_router_expert, b_router_expert, w_gate, w_up, w_down, g_ple,
                    w_ple_gate, w_ple_proj)
    bp = x_prompt.shape[0]
    s0 = jnp.zeros((DEPTH, bp, HG_HEADS, HG_DK, HG_DV), state_hgrn.dtype)
    c0 = jnp.zeros((DEPTH, bp, CONV_W - 1, SC_WIDTH), x_prompt.dtype)
    y_prompt, hgrn_prompt, conv_prompt = run_trunk(x_prompt, p_prompt, s0, c0, lbs, layer_params, g_final)
    y_sample, hgrn_sample, conv_sample = run_trunk(x_sample, p_sample, state_hgrn, state_conv, lbs,
                                                   layer_params, g_final)
    return (y_prompt, y_sample, hgrn_prompt, conv_prompt, hgrn_sample, conv_sample)


_drawn_inputs = setup_inputs


def setup_inputs(seed=0):
    import zlib

    import numpy as np

    out = dict(_drawn_inputs(seed))
    spreads = {}
    factors = {'g_hg_out': 21.247,
     'b_router_expert': 9.715,
     'g_ple': 64.0,
     'g_final': 31.052,
     'g_ffn': 5.115,
     'b_router_group': 8.0}
    for name, (base, spread) in spreads.items():
        noise = np.random.default_rng([zlib.crc32(name.encode()), seed]).standard_normal(out[name].shape)
        drawn = base * np.exp(spread * noise) if base else spread * noise
        out[name] = __import__('jax').numpy.asarray(drawn.astype(out[name].dtype))
    for name, factor in factors.items():
        out[name] = (out[name] * factor).astype(out[name].dtype)
    return out
```

```python
from contextlib import ExitStack

import numpy as np

import concourse.bass as bass
from concourse import mybir

F32 = mybir.dt.float32
I32 = mybir.dt.int32
U32 = mybir.dt.uint32
U8 = mybir.dt.uint8
ALU = mybir.AluOpType
ACT = mybir.ActivationFunctionType
AX = mybir.AxisListType

P = 128
D = 1024
KT = D // P
TP = 512
NB, TB = 8, 4
TS = NB * TB
T = TP + TS
HF = T // 2
TOK = [128, 128, 128, 128, TS]
NT = len(TOK)
NH, DK = 8, 128
GH = 4
NC = TP // P
LEV = 7
NE, NG, EG = 32, 4, 8
DE = 256
PLE = 256
EPS = 1e-6
CAP = 128
RANKS = 640
FAR = 1 << 20
UW = 2 + TP + NB * (TB + 2)
COL = dict(q=0, fg=1024, v=2048, og=3072, cb=4096, cc=5120, ch=6144, ga=7168, gb=8192)

MIX = [("hT", KT * T), ("X", GH * T), ("cum", GH * T), ("Q", GH * T), ("V", NT * 512), ("Kl", GH * T),
       ("Ql", GH * HF), ("A", GH * T), ("qc", GH * T), ("ktT", 5 * 512), ("U", GH * UW), ("C", KT * T),
       ("oT", KT * T), ("m", KT * T), ("S", GH * P), ("S0", 2 * NB * P), ("Vb", NB * P), ("tmp", 2 * T)]


def schedule():
    ev = [("xT", t) for t in range(NT)]

    def tiles(kind, g):
        return [(kind, j) for j in (range(NT) if kind == "v" else range(4 * g, 4 * g + 4))]

    def front(g):
        return [*tiles("fg", g), ("gates", g), *tiles("q", g), ("qprep", g),
                *[("v", (g, t)) for t in range(NT)]]

    def attention(g):
        steps = [[("kT", g), ("lev", (g, 0))]]
        for l in range(LEV):
            steps.append([("sc", (g, l))] + ([("lev", (g, l + 1))] if l + 1 < LEV else []))
        steps.append([("diag", g)])
        for h in range(4 * g, 4 * g + 4):
            steps += [[("stA", h)], [("stB", h)]]
        return steps

    def weave(steps, fill):
        out, n = [], 0
        for i, s in enumerate(steps):
            out += s
            upto = (i + 1) * len(fill) // len(steps)
            out += fill[n:upto]
            n = upto
        return out

    ev += front(0)
    ev += weave(attention(0), [x for g in range(2) for k in ("cc", "ch", "cb") for x in tiles(k, g)])
    ev += [("cvout", 0)]
    ev += front(1)
    ev += weave(attention(1), [("stat", j) for j in range(4)] + tiles("og", 0) + tiles("gb", 0) + tiles("yb", 0)
                + tiles("gb", 1) + tiles("yb", 1))
    ev += [("stat", j) for j in range(4, 8)] + tiles("og", 1)
    for g in range(2):
        ev += tiles("ga", g) + tiles("ya", g)
    return ev


TILE_KINDS = {"xT", "fg", "q", "v", "cc", "ch", "cb", "stat", "og", "gb", "yb", "ga", "ya"}


class Count:

    def __init__(self, by=1):
        self.n, self.by = 0, by

    def next(self):
        self.n += self.by
        return self.n


def layer(nc, a, o):
    ev = schedule()

    chunks, chunk_of, last_tile = [], {}, {}
    tile_no, n = {}, 0
    for kind, x in ev:
        if kind not in TILE_KINDS:
            continue
        tile_no[kind, x] = n
        if kind not in ("xT", "stat"):
            g = x[0] if kind == "v" else x // 4
            if kind in ("yb", "ya"):
                key = (kind, g, a["w_br_b" if kind == "yb" else "w_br_a"][0][:, 512 * g:512 * g + 512])
            else:
                key = (kind, g, a["w_in"][0][:, COL[kind] + 512 * g:COL[kind] + 512 * g + 512])
            if not chunks or chunks[-1][:2] != key[:2]:
                chunks.append(key)
            chunk_of[kind, x] = len(chunks) - 1
            last_tile[len(chunks) - 1] = n
        n += 1
    for c in range(2):
        chunks.append(("wo", c, a["w_out"][0][:, 512 * c:512 * c + 512]))
    wo_chunk = len(chunks) - 2
    wo_tile = n
    WO_T, H2_T, RT_T = 0, 1, 2
    ple_tile = wo_tile + 3 * NT

    bank_use, used = {}, {b: 0 for b in (4, 5, 6, 7)}

    def use(key, b):
        bank_use[key] = (b, used[b])
        used[b] += 1

    for kind, x in ev:
        if kind == "kT":
            for h in range(GH):
                use(("kT", x, h), 4 + h % 2)
            use(("kTs", x), 6)
        elif kind == "sc":
            for h in range(GH):
                use(("sc", x, h), 4 + h % 2)
        elif kind == "diag":
            for h in range(GH):
                use(("diag", x, h), 4 + h % 2)
            use(("diags", x), 6)
        elif kind == "stA":
            use(("inc", x), 4)
        elif kind == "stB":
            use(("o", x), 5)
            use(("os", x), 7)
            use(("si", x, 0), 6)
            use(("si", x, 1), 4)

    with ExitStack() as ctx:
        def sb(name, shape, dt=F32):
            return ctx.enter_context(nc.sbuf_tensor(name, shape, dt))

        def sem(name):
            return ctx.enter_context(nc.semaphore(name))

        W = sb("weights", [P, 2, KT, 512])
        arena = sb("arena", [P, sum(s for _, s in MIX)])
        R, at = {}, 0
        for name, size in MIX:
            R[name] = arena[:, at:at + size]
            R[name + "@"] = at
            at += size

        def area(off, size):
            return arena[:, off:off + size]

        hT = R["hT"].rearrange("p (k t) -> p k t", k=KT)
        X, cum, Q, A, qc, Kl = (R[k].rearrange("p (h t) -> p h t", h=GH) for k in ("X", "cum", "Q", "A", "qc", "Kl"))
        Ql = R["Ql"].rearrange("p (h t) -> p h t", h=GH)
        V = R["V"].rearrange("p (n d) -> p n d", n=NT)
        ktT = R["ktT"][:, 0:2048].rearrange("p (h c d) -> p h c d", h=GH, c=NC)
        ktTs = R["ktT"][:, 2048:2560].rearrange("p (h d) -> p h d", h=GH)
        U = R["U"].rearrange("p (j t) -> p j t", j=GH)
        SG = R["U"][:, 0:GH * T].rearrange("p (j t) -> p j t", j=GH)
        C, oT, m = (R[k].rearrange("p (k t) -> p k t", k=KT) for k in ("C", "oT", "m"))
        S = R["S"].rearrange("p (c d) -> p c d", c=NC)
        S0 = R["S0"].rearrange("p (s b d) -> p s b d", s=2, b=NB)
        Vb = R["Vb"].rearrange("p (b d) -> p b d", b=NB)
        tmp = R["tmp"].rearrange("p (s t) -> p s t", s=2)
        xt = area(R["C@"], NT * D).rearrange("p (n d) -> p n d", n=NT)
        cs = area(R["m@"], D)
        tab0 = area(R["m@"] + D, NE * RANKS * 4 // P).bitcast(I32)

        ident = sb("ident", [P, P])
        ones = sb("ones", [P, P])
        lmask = sb("level_masks", [P, LEV, 256], U8)
        smask = sb("sample_masks", [TS, 2, 16], U8)
        small = sb("small_consts", [P, 64])
        bmask, iota, tokno = small[:, 0:8], small[:, 8:40], small[:, 40:45]
        keep = sb("scan_keep", [P, TS])
        lmask_f = area(R["m@"] + 2 * D + P, LEV * 256)
        smask_f = area(R["m@"] + 2 * D + P + LEV * 256, 32)[0:TS]
        rows = area(R["m@"] + 2 * D, P)[0:48, :]
        gain = sb("gain_cols", [P, 48])
        cst = sb("conv_hist", [P, KT, 16])
        ul = sb("conv_tail", [P, KT, 18])
        ss = sb("sum_sq", [P, NT])
        rs = sb("rstd", [P, NT])
        El = sb("exp_last", [P, GH, NC + NB])
        eps = sb("eps", [P, 2])
        tails = area(R["tmp@"], D)

        ew = [area(i * 6144, 6144) for i in range(2)]
        wgu = [e[:, 0:4096].rearrange("p (k n) -> p k n", k=KT) for e in ew]
        wdn = [e[:, 4096:6144].rearrange("p (k n) -> p k n", k=2) for e in ew]
        at = R["V@"] + NT * 512
        x1 = area(at, NT * D).rearrange("p (n d) -> p n d", n=NT)
        at += NT * D
        h2 = [area(at + i * D, D) for i in range(2)]
        h2T = area(at + 2 * D, D).rearrange("p (k t) -> p k t", k=KT)
        at += 3 * D
        xg = [area(at + i * D, D) for i in range(2)]
        xgT = [area(at + (2 + i) * D, D).rearrange("p (k t) -> p k t", k=KT) for i in range(2)]
        h3 = [area(at + i * D, D) for i in range(2)]
        h3T = [area(at + (2 + i) * D, D).rearrange("p (k t) -> p k t", k=KT) for i in range(2)]
        s3, out3 = [area(i * D, D) for i in range(2)], [area((2 + i) * D, D) for i in range(2)]
        squares = area(10 * D, D)
        at += 4 * D
        sg = [area(at + i * 256, 256) for i in range(2)]
        hid = [area(at + (2 + i) * 256, 256) for i in range(2)]
        hidT = [area(at + (4 + i) * 256, 256).rearrange("p (k t) -> p k t", k=2) for i in range(2)]
        at += 6 * 256
        yo = [area(at + i * D, D) for i in range(2)]
        at += 2 * D
        assert at <= R["oT@"]
        yk_at = [R["oT@"] + i * D for i in range(4)] + [(4 + i) * D for i in range(2 * NT - 4)]
        assert yk_at[-1] + D <= 10 * D and 11 * D <= 2 * 6144
        yk = [[area(yk_at[2 * t + k], D) for k in range(2)] for t in range(NT)]
        at = R["m@"]
        pt = area(at, NT * PLE).rearrange("p (n d) -> p n d", n=NT)
        pT = area(at + NT * PLE, 2 * T).rearrange("p (k t) -> p k t", k=2)
        at = R["S@"]
        wpp = area(at, 2 * D).rearrange("p (k n) -> p k n", k=2)
        gffn, gfin = area(at + 2 * D, D), area(at + 3 * D, D)
        at += 4 * D
        wr = area(at, KT * 36).rearrange("p (k n) -> p k n", k=KT)
        at += KT * 36
        M = area(at, NT * NE).rearrange("p (t e) -> p t e", t=NT)
        at += NT * NE
        tb = area(at, NE * 4).bitcast(I32).rearrange("p (e c) -> p e c", e=NE)
        at += NE * 4
        assert at <= R["tmp@"] + 2 * T
        at = R["hT@"] + 2 * 6144
        lg = area(at, 36)
        rb = area(at + 36, 36)
        g8, sel, rf = area(at + 72, 8), area(at + 80, 8), area(at + 88, 16)
        top = area(at + 104, 16).rearrange("p (k n) -> p k n", k=2)
        topi = area(at + 120, 16).bitcast(U32).rearrange("p (k n) -> p k n", k=2)
        oh = area(at + 136, 2 * NE).rearrange("p (k e) -> p k e", k=2)
        junk = area(at + 200, NE)
        slot = area(at + 232, 2 * NT).bitcast(I32).rearrange("p (t k) -> p t k", k=2)
        rec = area(at + 242, 8 * NT).bitcast(I32).rearrange("p (t k c) -> p t k c", t=NT, k=2)
        gidx = [area(at + 282 + i, 1).bitcast(I32) for i in range(2)]
        sidx = [area(at + 284 + i, 1).bitcast(I32) for i in range(2)]
        tri = area(at + 286, P)
        ftab = area(at + 414, 4).bitcast(I32)
        flag = area(at + 418, 1)[0:1].bitcast(I32)
        assert at + 419 <= R["V@"] + NT * 512

        ps = ctx.enter_context(nc.psum_tensor("ps", [P, 8, 512], F32))

        h2_dram = nc.dram_tensor("h2_rows", [T, D], F32).ap()
        y_dram = nc.dram_tensor("expert_rows", [2 * T, D], F32).ap()
        tab_dram = nc.dram_tensor("route_table", [NE * RANKS, 4], I32).ap()

        tile_ready = [sem(f"tile_ready{p}") for p in range(2)]
        tile_freed = [sem(f"tile_freed{p}") for p in range(2)]
        bank_ready = {b: sem(f"bank_ready{b}") for b in used}
        bank_freed = {b: sem(f"bank_freed{b}") for b in used}
        w_loaded = [sem(f"w_loaded{s}") for s in range(2)]
        x_loaded = [sem(f"x_loaded{t}") for t in range(NT)]
        id_loaded, c_loaded, rows_loaded = sem("ident_loaded"), sem("consts_loaded"), sem("rows_loaded")
        rows_ready, rows_freed = sem("rows_ready"), sem("rows_freed")
        pool_set = sem("pool_set")
        act_step, dve_step, pool_step = sem("act_step"), sem("dve_step"), sem("pool_step")
        a2d, d2a = sem("act_to_dve"), sem("dve_to_act")
        d2p = sem("dve_to_pe")
        kt_ready, lev_ready, vb_ready = sem("kt_ready"), sem("lev_ready"), sem("vb_ready")
        a2p = sem("act_to_pe")
        p2d = sem("pool_to_dve")
        kl_zeroed = sem("kl_zeroed")
        s0_loaded = [sem(f"s0_loaded{i}") for i in range(2)]
        s0_out, s_out = [sem(f"s0_out{i}") for i in range(2)], sem("s_out")
        dve_state = sem("dve_state")
        x1_loaded, r_loaded = sem("x1_loaded"), sem("router_loaded")
        tab_ready, tab_set = sem("empty_table_ready"), sem("table_set")
        tails_ready, tails_out = sem("tails_ready"), sem("tails_out")

        def waits_tile(eng, kind, x):
            n = tile_no[kind, x]
            eng.wait_ge(tile_ready[n % 2], n // 2 + 1)
            return 2 * (n % 2), tile_freed[n % 2]

        def after_tile(eng, kind, x):
            n = tile_no[kind, x]
            eng.wait_ge(tile_freed[n % 2], n // 2 + 1)

        def full(eng, key):
            b, i = bank_use[key]
            eng.wait_ge(bank_ready[b], i + 1)
            return b, bank_freed[b]

        def after_banks(eng, keys):
            last = {}
            for key in keys:
                b, i = bank_use[key]
                last[b] = i + 1
            for b, i in last.items():
                eng.wait_ge(bank_freed[b], i)

        def halves(b):
            return ps[:, b:b + 2, 0:HF]

        def split(x):
            return x.rearrange("p (s t) -> p s t", s=2)

        def tok(t):
            return slice(t * P, t * P + TOK[t])

        def lvl(x, l, heads=True):
            hs = 64 >> l
            if hs <= 2:
                return x.rearrange("p h (b two i) -> p (h b) two i", two=2, i=hs)
            return x[:, :, 0:TP].rearrange("p h (b two i) -> p h b two i", two=2, i=hs)

        def lvq(l):
            hs = 64 >> l
            if hs <= 2:
                return Ql.rearrange("p h (b i) -> p (h b) i", i=hs)
            return Ql[:, :, 0:256].rearrange("p h (b i) -> p h b i", i=hs)

        with nc.Block() as block:

            @block.sync
            def _(sp):
                sp.dma_start(ident[:, :], a["c_ident"]).then_inc(id_loaded, 16)
                for t in range(NT):
                    src = a["x_prompt"][0, t * P:t * P + P, :] if t < 4 else a["x_sample"].rearrange("b t d -> (b t) d")
                    sp.dma_start(xt[0:TOK[t], t, :], src).then_inc(x_loaded[t], 16)
                for i, (name, r0) in enumerate((("g_mix", 0), ("g_hg_out", 8), ("g_ple", 16))):
                    sp.dma_start(rows[r0:r0 + 8, :], a[name].rearrange("o (r p) -> (o r) p", p=P)).then_inc(rows_loaded, 16)
                sp.dma_start(rows[24:48, :], a["w_conv"].rearrange("o j (r p) -> (o j r) p", p=P)).then_inc(rows_loaded, 16)
                sp.dma_start(cs[0:16, :], a["state_conv"].rearrange("o b j c -> (o b j) c")).then_inc(rows_loaded, 16)
                n_chunk = [0]

                def load_chunk():
                    c = n_chunk[0]
                    n_chunk[0] += 1
                    if c >= 2:
                        last = last_tile[c - 2]
                        sp.wait_ge(tile_ready[last % 2], last // 2 + 1)
                    sp.dma_start(W[:, c % 2], chunks[c][2].rearrange("(k p) n -> p k n", p=P)).then_inc(w_loaded[c % 2], 16)

                load_chunk()
                sp.dma_start(small[:, :], a["c_small"]).then_inc(c_loaded, 16)
                sp.dma_start(lmask_f, a["c_lmask"].rearrange("p l t -> p (l t)")).then_inc(c_loaded, 16)
                sp.dma_start(smask_f, a["c_smask"].rearrange("p l t -> p (l t)")).then_inc(c_loaded, 16)
                load_chunk()
                sp.wait_ge(tab_ready, 1)
                sp.dma_start(tab_dram.rearrange("(p r) c -> p (r c)", p=P), tab0).then_inc(tab_set, 16)
                first_use = {c: min(i for i, e in enumerate(ev) if chunk_of.get(e) == c) for c in range(wo_chunk)}
                for i, (kind, x) in enumerate(ev):
                    if n_chunk[0] < len(chunks) and first_use.get(n_chunk[0] - 1, len(ev)) == i:
                        load_chunk()
                    if kind == "stA":
                        h, s = x, x % 2
                        if h >= 2:
                            sp.wait_ge(s0_out[s], 16 * (h // 2))
                        sp.dma_start(S0[:, s], a["state_hgrn"][0, :, h].rearrange("b k v -> k b v")).then_inc(s0_loaded[s], 16)
                    if kind == "stB":
                        h, s = x, x % 2
                        sp.wait_ge(dve_state, 2 * h + 1)
                        sp.dma_start(o["hgrn_prompt"][0, 0, h], S[:, NC - 1, :]).then_inc(s_out, 16)
                        sp.wait_ge(dve_state, 2 * h + 2)
                        sp.dma_start(o["hgrn_sample"][0, :, h].rearrange("b k v -> k b v"), S0[:, s]).then_inc(s0_out[s], 16)
                    if kind == "cvout":
                        sp.wait_ge(tails_ready, 1)
                        sp.dma_start(o["conv_prompt"][0, 0], tails[0:2, :]).then_inc(tails_out, 16)
                        sp.dma_start(o["conv_sample"][0].rearrange("b j c -> (b j) c"), tails[2:18, :]).then_inc(tails_out, 16)
                while n_chunk[0] < len(chunks):
                    load_chunk()
                for t in range(NT):
                    src = a["x_prompt"][0, t * P:t * P + P, :] if t < 4 else a["x_sample"].rearrange("b t d -> (b t) d")
                    sp.dma_start(x1[0:TOK[t], t, :], src).then_inc(x1_loaded, 16)
                with nc.allow_non_contiguous_dma(reason="router weights"):
                    sp.dma_start(wr[:, :, 0:4], a["w_router_group"][0].rearrange("(k p) n -> p k n", p=P)).then_inc(r_loaded, 16)
                    sp.dma_start(wr[:, :, 4:36], a["w_router_expert"][0].rearrange("(k p) n -> p k n", p=P)).then_inc(r_loaded, 16)
                sp.dma_start(rb[:, 0:4], a["b_router_group"].to_broadcast([P, 4])).then_inc(r_loaded, 16)
                sp.dma_start(rb[:, 4:36], a["b_router_expert"].to_broadcast([P, 32])).then_inc(r_loaded, 16)
                sp.dma_start(tri, a["c_tri"]).then_inc(r_loaded, 16)
                sp.dma_start(gffn, a["g_ffn"].to_broadcast([P, D])).then_inc(r_loaded, 16)
                sp.dma_start(gfin, a["g_final"].unsqueeze(0).to_broadcast([P, D])).then_inc(r_loaded, 16)
                sp.wait_ge(s_out, 16 * NH)
                sp.wait_ge(s0_out[0], 16 * 4)
                sp.wait_ge(s0_out[1], 16 * 4)
                sp.wait_ge(tails_out, 32)

            @block.gpsimd
            def _(pool):
                nc.gpsimd.memset(A, 0.0).then_inc(pool_set, 1)
                nc.gpsimd.memset(tab0, FAR).then_inc(pool_step, 1)
                pool.wait_ge(pool_step, 1)
                nc.gpsimd.memset(tab0.rearrange("p (r c) -> p r c", c=4)[:, :, 2:4], 0).then_inc(tab_ready, 1)
                for kind, x in ev:
                    if kind == "lev":
                        g, l = x
                        if l:
                            full(pool, ("sc", (g, l - 1), 3))
                        else:
                            for h in range(GH):
                                full(pool, ("kT", g, h))
                            full(pool, ("kTs", g))
                        v = lvl(Kl, l)
                        v = v[:, :, 1, :] if len(v.shape) == 4 else v[:, :, :, 1, :]
                        nc.gpsimd.memset(v, 0.0).then_inc(kl_zeroed, 1)

            @block.scalar
            def _(act):
                step, d2a_n = Count(), Count()

                def link(ins):
                    ins.then_inc(act_step, 1)
                    act.wait_ge(act_step, step.next())

                def from_dve():
                    act.wait_ge(d2a, d2a_n.next())

                def rms(src, dst, scale):
                    link(nc.scalar.activation(dst, src, ACT.Ln, bias=eps[0:dst.shape[0], 0:1], scale=scale))
                    return nc.scalar.activation(dst, dst, ACT.Exp, scale=-0.5)

                from_dve()
                for kind, x in ev:
                    if kind == "xT":
                        n = TOK[x]
                        act.wait_ge(x_loaded[x], 16)
                        link(nc.scalar.activation(R["X"][0:n, 0:D], xt[0:n, x, :], ACT.Square, accum_out=ss[0:n, x:x + 1]))
                        rms(ss[0:n, x:x + 1], rs[0:n, x:x + 1], 1.0 / D).then_inc(a2d, 1)
                    elif kind == "fg":
                        b, freed = waits_tile(act, kind, x)
                        if x >= 4:
                            for h in range(GH):
                                full(act, ("diag", 0, h))
                            full(act, ("diags", 0))
                        nc.scalar.activation(split(X[:, x % 4, :]), halves(b), ACT.Copy).then_inc(freed, 1)
                    elif kind in ("q", "og"):
                        b, freed = waits_tile(act, kind, x)
                        from_dve()
                        nc.scalar.activation(split(tmp[:, x % 2, :]), halves(b), ACT.Tanh, scale=0.5).then_inc(a2d, 1)
                    elif kind == "v":
                        b, freed = waits_tile(act, kind, x)
                        g, t = x
                        if g:
                            for bank in (("o", 3), ("os", 3), ("si", 3, 0), ("si", 3, 1)):
                                full(act, bank)
                        nc.scalar.activation(V[0:TOK[t], t, :], ps[0:TOK[t], b, :], ACT.Copy).then_inc(freed, 1)
                    elif kind == "gates":
                        from_dve()
                        link(nc.scalar.activation(qc, qc, ACT.Exp))
                        nc.scalar.activation(Kl, qc, ACT.Ln, bias=eps[:, 1:2]).then_inc(a2d, 1)
                        from_dve()
                        nc.scalar.activation(X, X, ACT.Exp).then_inc(a2d, 1)
                    elif kind == "qprep":
                        from_dve()
                        nc.scalar.activation(qc, cum, ACT.Exp).then_inc(a2d, 1)
                        nc.scalar.activation(El[:, :, 0:NC], cum[:, :, P - 1:TP:P], ACT.Exp).then_inc(a2d, 1)
                        nc.scalar.activation(El[:, :, NC:NC + NB], cum[:, :, TP + TB - 1:T:TB], ACT.Exp).then_inc(a2d, 1)
                        from_dve()
                        nc.scalar.activation(Kl, Kl, ACT.Exp).then_inc(a2d, 1)
                    elif kind == "kT":
                        for h in range(GH):
                            b, freed = full(act, ("kT", x, h))
                            nc.scalar.activation(ktT[:, h], ps[:, b, :].rearrange("p (c d) -> p c d", c=NC),
                                                 ACT.Copy).then_inc(freed, 1)
                        b, freed = full(act, ("kTs", x))
                        nc.scalar.activation(ktTs[0:TS], ps[0:TS, b, :].rearrange("p (h d) -> p h d", h=GH),
                                             ACT.Copy).then_inc(freed, 1)
                    elif kind == "lev":
                        g, l = x
                        from_dve()
                        q = lvq(l)
                        nc.scalar.activation(q, q, ACT.Exp).then_inc(a2d, 1)
                        from_dve()
                        k = lvl(Kl, l)
                        k = k[:, :, 0, :] if len(k.shape) == 4 else k[:, :, :, 0, :]
                        nc.scalar.activation(k, k, ACT.Exp).then_inc(a2d, 1)
                    elif kind == "stB":
                        b, freed = full(act, ("o", x))
                        nc.scalar.activation(oT[:, x, 0:TP], ps[:, b, :], ACT.Copy).then_inc(freed, 1)
                        b, freed = full(act, ("os", x))
                        nc.scalar.activation(oT[:, x, TP:T], ps[:, b, 0:TS], ACT.Copy).then_inc(freed, 1)
                    elif kind == "cc":
                        b, freed = waits_tile(act, kind, x)
                        nc.scalar.activation(split(C[:, x, :]), halves(b), ACT.Copy).then_inc(freed, 1)
                    elif kind == "ch":
                        j = x % 4
                        u = U[:, j, :]
                        from_dve()
                        nc.scalar.activation(u[:, 2:2 + TP], C[:, x, 0:TP], ACT.Copy).then_inc(a2d, 1)
                        us = u[:, 2 + TP:UW].rearrange("p (b t) -> p b t", b=NB)
                        nc.scalar.activation(us[:, :, 2:2 + TB], C[:, x, TP:T].rearrange("p (b t) -> p b t", b=NB),
                                             ACT.Copy).then_inc(a2d, 1)
                        nc.scalar.activation(us[:, :, 0:2], cst[:, x, :].rearrange("p (b t) -> p b t", b=NB),
                                             ACT.Copy).then_inc(a2d, 1)
                        nc.scalar.activation(ul[:, x, 0:2], C[:, x, TP - 2:TP], ACT.Copy).then_inc(a2d, 1)
                        nc.scalar.activation(ul[:, x, 2:18].rearrange("p (b t) -> p b t", b=NB),
                                             C[:, x, TP:T].rearrange("p (b t) -> p b t", b=NB)[:, :, 2:4],
                                             ACT.Copy).then_inc(a2d, 1)
                    elif kind == "stat":
                        b, freed = waits_tile(act, kind, x)
                        from_dve()
                        link(nc.scalar.activation(split(tmp[:, x % 2, :]), halves(b), ACT.Ln, bias=eps[:, 0:1],
                                                  scale=1.0 / P))
                        nc.scalar.activation(tmp[:, x % 2, :], tmp[:, x % 2, :], ACT.Exp, scale=-0.5).then_inc(a2d, 1)
                    elif kind in ("gb", "ga"):
                        b, freed = waits_tile(act, kind, x)
                        from_dve()
                        nc.scalar.activation(split(SG[:, x % 4, :]), halves(b), ACT.Tanh, scale=0.5).then_inc(freed, 1)

            @block.vector
            def _(dve):
                v = nc.vector
                step, a2d_n = Count(), Count()

                def link(ins):
                    ins.then_inc(dve_step, 1)
                    dve.wait_ge(dve_step, step.next())

                def from_act():
                    dve.wait_ge(a2d, a2d_n.next())

                def sigmoid(x):
                    return v.tensor_scalar(x, x, 0.5, 0.5, ALU.mult, ALU.add)

                link(v.memset(eps[:, 0:1], EPS))
                link(v.memset(eps[:, 1:2], 1.0))
                link(v.memset(keep[:, :], 1.0))
                link(v.memset(keep[:, 0:TS:TB], 0.0))
                v.memset(ones[:, :], 1.0).then_inc(d2a, 1)
                dve.wait_ge(d2a, 1)
                dve.wait_ge(pool_set, 1)
                dve.wait_ge(id_loaded, 16)
                dve.wait_ge(c_loaded, 48)
                link(v.tensor_copy(lmask[:, :, :].rearrange("p l t -> p (l t)"), lmask_f))
                link(v.tensor_copy(smask[:, :, :].rearrange("p l t -> p (l t)"), smask_f))
                for kind, x in ev:
                    if kind == "xT":
                        n = TOK[x]
                        from_act()
                        dve.wait_ge(x_loaded[x], 16)
                        v.tensor_scalar(xt[0:n, x, :], xt[0:n, x, :], rs[0:n, x:x + 1], None, ALU.mult).then_inc(d2p, 1)
                        if x == 0:
                            dve.wait_ge(rows_ready, 1)
                            v.tensor_copy(gain[:, :], ps[:, 4, 0:48]).then_inc(rows_freed, 1)
                            dve.wait_ge(rows_ready, 2)
                            v.tensor_copy(cst[:, :, :], ps[:, 5, 0:128].rearrange("p (k c) -> p k c", k=KT)).then_inc(rows_freed, 1)
                            dve.wait_ge(rows_freed, 2)
                        b, freed = waits_tile(dve, kind, x)
                        v.tensor_tensor(hT[:, :, tok(x)],
                                        ps[:, b:b + 2, :].rearrange("p s (k t) -> p (s k) t", k=4)[:, :, 0:n],
                                        gain[:, 0:8].unsqueeze(2).to_broadcast([P, 8, n]), ALU.mult).then_inc(freed, 1)
                    elif kind == "gates":
                        for h in range(GH):
                            after_tile(dve, "fg", 4 * x + h)
                        if x:
                            full(dve, ("o", 3)), full(dve, ("os", 3))
                        v.scalar_tensor_tensor(R["qc"], R["X"], -1.0, R["X"], ALU.mult, ALU.min).then_inc(d2a, 1)
                        from_act()
                        link(v.scalar_tensor_tensor(R["qc"], R["X"], 0.0, R["Kl"], ALU.min, ALU.subtract))
                        v.tensor_tensor(X, qc, X, ALU.subtract).then_inc(d2a, 1)
                        last = None
                        for h in range(GH):
                            for c in range(NC):
                                s = slice(c * P, c * P + P)
                                v.tensor_tensor_scan(cum[:, h, s], ones[:, :], qc[:, h, s], 0.0, ALU.mult,
                                                     ALU.add).then_inc(dve_step, 1)
                                step.next()
                            v.tensor_tensor_scan(cum[:, h, TP:T], keep[:, :], qc[:, h, TP:T], 0.0, ALU.mult,
                                                 ALU.add).then_inc(dve_step, 1)
                            step.next()
                        from_act()
                    elif kind in ("q", "og"):
                        b, freed = waits_tile(dve, kind, x)
                        v.engine_nop().then_inc(d2a, 1)
                        from_act()
                        link(sigmoid(tmp[:, x % 2, :]))
                        if kind == "q":
                            v.tensor_tensor(split(Q[:, x % 4, :]), split(tmp[:, x % 2, :]), halves(b), ALU.mult).then_inc(freed, 1)
                            after_tile(dve, kind, x)
                        else:
                            link(v.tensor_tensor(split(tmp[:, x % 2, :]), split(tmp[:, x % 2, :]), halves(b), ALU.mult))
                            v.tensor_tensor(oT[:, x, :], oT[:, x, :], tmp[:, x % 2, :], ALU.mult).then_inc(freed, 1)
                            after_tile(dve, kind, x)
                    elif kind == "qprep":
                        dve.wait_ge(dve_step, step.n)
                        v.engine_nop().then_inc(d2a, 1)
                        last = cum[:, :, P - 1:TP:P]
                        link(v.tensor_tensor(Kl[:, :, 0:TP].rearrange("p h (c s) -> p h c s", s=P),
                                             last.unsqueeze(3).to_broadcast([P, GH, NC, P]),
                                             cum[:, :, 0:TP].rearrange("p h (c s) -> p h c s", s=P), ALU.subtract))
                        last = cum[:, :, TP + TB - 1:T:TB]
                        v.tensor_tensor(Kl[:, :, TP:T].rearrange("p h (c s) -> p h c s", s=TB),
                                        last.unsqueeze(3).to_broadcast([P, GH, NB, TB]),
                                        cum[:, :, TP:T].rearrange("p h (c s) -> p h c s", s=TB),
                                        ALU.subtract).then_inc(d2a, 1)
                        from_act()
                        link(v.tensor_tensor(qc, qc, Q, ALU.mult))
                        from_act(), from_act(), from_act()
                        v.tensor_tensor(Kl, Kl, X, ALU.mult).then_inc(kt_ready, 1)
                    elif kind == "lev":
                        g, l = x
                        hs = 64 >> l
                        if l:
                            full(dve, ("sc", (g, l - 1), 3))
                        else:
                            for h in range(GH):
                                full(dve, ("kT", g, h))
                            full(dve, ("kTs", g))
                        c4, k4, x4, q4, Q4 = lvl(cum, l), lvl(Kl, l), lvl(X, l), lvq(l), lvl(Q, l)
                        one, two = ((lambda y: y[:, :, 0, :]), (lambda y: y[:, :, 1, :])) if hs <= 2 else \
                            ((lambda y: y[:, :, :, 0, :]), (lambda y: y[:, :, :, 1, :]))
                        mid = one(c4)[..., hs - 1:hs].to_broadcast(list(one(c4).shape))
                        v.tensor_tensor(q4, two(c4), mid, ALU.subtract).then_inc(d2a, 1)
                        dve.wait_ge(kl_zeroed, LEV * g + l + 1)
                        v.tensor_tensor(one(k4), mid, one(c4), ALU.subtract).then_inc(d2a, 1)
                        from_act()
                        v.tensor_tensor(q4, q4, two(Q4), ALU.mult).then_inc(lev_ready, 1)
                        from_act()
                        v.tensor_tensor(one(k4), one(k4), one(x4), ALU.mult).then_inc(lev_ready, 1)
                    elif kind == "sc":
                        g, l = x
                        hs = 64 >> l
                        for h in range(GH):
                            if l == 0 and h == 0 and g:
                                full(dve, ("o", 3)), full(dve, ("os", 3))
                            b, freed = full(dve, ("sc", x, h))
                            dst = A[:, h, 0:TP].rearrange("p (b two i) -> p b two i", two=2, i=hs)[:, :, 1, :]
                            ins = v.copy_predicated(dst, lmask[:, l, :].rearrange("p (b i) -> p b i", i=hs),
                                                    ps[:, b, 0:256].rearrange("p (b i) -> p b i", i=hs))
                            if hs <= 2:
                                link(ins)
                                dst = A[0:TS, h, TP:T].rearrange("p (b two i) -> p b two i", two=2, i=hs)[:, :, 1, :]
                                ins = v.copy_predicated(dst, smask[:, l - 5, :].rearrange("p (b i) -> p b i", i=hs),
                                                        ps[0:TS, b, 256:272].rearrange("p (b i) -> p b i", i=hs))
                            ins.then_inc(freed, 1)
                        after_banks(dve, [("sc", x, h) for h in range(GH)])
                    elif kind == "diag":
                        for h in range(GH):
                            b, freed = full(dve, ("diag", x, h))
                            v.copy_predicated(A[:, h, 0:TP].rearrange("p (c t) -> p c t", c=NC),
                                              ident[:, :].bitcast(U32).unsqueeze(1).to_broadcast([P, NC, P]),
                                              ps[:, b, :].rearrange("p (c t) -> p c t", c=NC)).then_inc(freed, 1)
                        b, freed = full(dve, ("diags", x))
                        v.copy_predicated(A[0:TS, :, TP:T],
                                          ident[0:TS, 0:TS].bitcast(U32).unsqueeze(1).to_broadcast([TS, GH, TS]),
                                          ps[0:TS, b, 0:GH * TS].rearrange("p (h t) -> p h t", h=GH)).then_inc(freed, 1)
                    elif kind == "stA":
                        h = x % 4
                        if x:
                            full(dve, ("o", x - 1))
                            dve.wait_ge(s_out, 16 * x)
                            for i in range(2):
                                full(dve, ("si", x - 1, i))
                        b, freed = full(dve, ("inc", x))
                        link(v.tensor_copy(S[:, 0, :], ps[:, b, 0:P]))
                        for c in range(1, NC):
                            ins = v.scalar_tensor_tensor(S[:, c, :], S[:, c - 1, :], El[:, h, c:c + 1],
                                                         ps[:, b, c * P:c * P + P], ALU.mult, ALU.add)
                            if c < NC - 1:
                                link(ins)
                        ins.then_inc(freed, 1)
                        v.tensor_tensor(Vb[0:TS], V[0:TS, 4, h * P:h * P + P].unsqueeze(1).to_broadcast([TS, NB, P]),
                                        bmask[0:TS, :].unsqueeze(2).to_broadcast([TS, NB, P]), ALU.mult).then_inc(vb_ready, 1)
                        b, i = bank_use["inc", x]
                        dve.wait_ge(bank_freed[b], i + 1)
                        v.engine_nop().then_inc(dve_state, 1)
                    elif kind == "stB":
                        h, s = x % 4, x % 2
                        full(dve, ("os", x))
                        dec = El[:, h, NC:NC + NB].unsqueeze(2).to_broadcast([P, NB, P])
                        link(v.tensor_tensor(S0[:, s], S0[:, s], dec, ALU.mult))
                        for i in range(2):
                            b, freed = full(dve, ("si", x, i))
                            y = S0[:, s, 4 * i:4 * i + 4, :]
                            v.tensor_tensor(y, y, ps[:, b, :].rearrange("p (b d) -> p b d", b=4), ALU.add).then_inc(freed, 1)
                        after_banks(dve, [("si", x, 0), ("si", x, 1)])
                        v.engine_nop().then_inc(dve_state, 1)
                    elif kind == "ch":
                        b, freed = waits_tile(dve, kind, x)
                        after_tile(dve, "cc", x)
                        j = x % 4
                        u = U[:, j, :]
                        us = u[:, 2 + TP:UW].rearrange("p (b t) -> p b t", b=NB)
                        v.tensor_tensor(split(C[:, x, :]), split(C[:, x, :]), halves(b), ALU.mult).then_inc(freed, 1)
                        after_tile(dve, kind, x)
                        link(v.memset(u[:, 0:2], 0.0))
                        v.engine_nop().then_inc(d2a, 1)
                        for _ in range(5):
                            from_act()
                        cv = C[:, x, 0:TP]
                        cvs = C[:, x, TP:T].rearrange("p (b t) -> p b t", b=NB)
                        w = [gain[:, 24 + 8 * i + x:25 + 8 * i + x] for i in range(3)]
                        link(v.tensor_scalar(cv, u[:, 0:TP], w[0], None, ALU.mult))
                        link(v.tensor_scalar(cvs, us[:, :, 0:TB], w[0], None, ALU.mult))
                        for i in (1, 2):
                            link(v.scalar_tensor_tensor(cv, u[:, i:i + TP], w[i], cv, ALU.mult, ALU.add))
                            link(v.scalar_tensor_tensor(cvs, us[:, :, i:i + TB], w[i], cvs, ALU.mult, ALU.add))
                    elif kind == "cb":
                        b, freed = waits_tile(dve, kind, x)
                        v.tensor_tensor(split(C[:, x, :]), split(C[:, x, :]), halves(b), ALU.mult).then_inc(freed, 1)
                    elif kind == "cvout":
                        after_tile(dve, "cb", 6), after_tile(dve, "cb", 7)
                        v.engine_nop().then_inc(d2p, 1)
                        dve.wait_ge(rows_ready, 3)
                        link(v.tensor_copy(tails[0:18, 0:512], ps[0:18, 6, :]))
                        v.tensor_copy(tails[0:18, 512:1024], ps[0:18, 7, :]).then_inc(tails_ready, 1)
                        dve.wait_ge(tails_ready, 1)
                        dve.wait_ge(tails_out, 32)
                    elif kind == "stat":
                        b5, b7 = bank_use["o", x], bank_use["os", x]
                        dve.wait_ge(bank_freed[5], b5[1] + 1), dve.wait_ge(bank_freed[7], b7[1] + 1)
                        if x % 4 >= 2:
                            after_tile(dve, "stat", x - 2)
                        v.tensor_tensor(SG[:, x % 2, :], oT[:, x, :], oT[:, x, :], ALU.mult).then_inc(d2p, 1)
                        v.engine_nop().then_inc(d2a, 1)
                        b, freed = waits_tile(dve, kind, x)
                        from_act()
                        v.scalar_tensor_tensor(oT[:, x, :], oT[:, x, :], gain[:, 8 + x:9 + x], tmp[:, x % 2, :],
                                               ALU.mult, ALU.mult).then_inc(freed, 1)
                        after_tile(dve, kind, x)
                    elif kind in ("gb", "ga"):
                        v.engine_nop().then_inc(d2a, 1)
                        after_tile(dve, kind, x)
                        link(sigmoid(SG[:, x % 4, :]))
                    elif kind == "yb":
                        b, freed = waits_tile(dve, kind, x)
                        v.tensor_tensor(split(m[:, x, :]), split(SG[:, x % 4, :]), halves(b), ALU.mult).then_inc(freed, 1)
                        after_tile(dve, kind, x)
                    elif kind == "ya":
                        b, freed = waits_tile(dve, kind, x)
                        link(v.tensor_tensor(split(SG[:, x % 4, :]), split(SG[:, x % 4, :]), halves(b), ALU.mult))
                        v.tensor_tensor(m[:, x, :], m[:, x, :], SG[:, x % 4, :], ALU.add).then_inc(freed, 1)
                        after_tile(dve, kind, x)

            @block.tensor
            def _(pe):
                mm, tr = nc.tensor.matmul, nc.tensor.transpose
                d2p_n = Count()

                def from_dve():
                    pe.wait_ge(d2p, d2p_n.next())

                def empty(key):
                    b, i = bank_use[key]
                    if i:
                        pe.wait_ge(bank_freed[b], i)
                    return b

                pe.wait_ge(id_loaded, 16)
                pe.wait_ge(rows_loaded, 80)
                tr(ps[:, 4, 0:48], rows[:, :], ident[0:48, 0:48]).then_inc(rows_ready, 1)
                for k in range(KT):
                    ins = tr(ps[:, 5, 16 * k:16 * k + 16], cs[0:16, k * P:k * P + P], ident[0:16, 0:16])
                ins.then_inc(rows_ready, 1)
                pe.wait_ge(rows_freed, 2)
                tails_seen = False
                for kind, x in ev:
                    if kind in TILE_KINDS:
                        n = tile_no[kind, x]
                        b = 2 * (n % 2)
                        if n >= 2:
                            pe.wait_ge(tile_freed[n % 2], n // 2)
                    if kind == "xT":
                        r = TOK[x]
                        from_dve()
                        for k in range(KT):
                            ins = tr(ps[:, b + k // 4, (k % 4) * P:(k % 4) * P + r], xt[0:r, x, k * P:k * P + P],
                                     ident[0:r, 0:r])
                        ins.then_inc(tile_ready[n % 2], 1)
                    elif kind in COL and kind != "v" or kind in ("yb", "ya"):
                        if (kind, x) == ("fg", 0):
                            for t in range(NT):
                                after_tile(pe, "xT", t)
                        if (kind, x) == ("yb", 0):
                            for j in range(KT):
                                after_tile(pe, "cb", j)
                        if (kind, x) == ("ya", 0):
                            for j in range(KT):
                                after_tile(pe, "og", j)
                        c = chunk_of[kind, x]
                        pe.wait_ge(w_loaded[c % 2], 16 * (c // 2 + 1))
                        src = {"yb": C, "ya": oT}.get(kind, hT)
                        col = (x % 4) * P
                        for k in range(KT):
                            for s in range(2):
                                ins = mm(ps[:, b + s, 0:HF], W[:, c % 2, k, col:col + P], src[:, k, s * HF:s * HF + HF],
                                         start=(k == 0), stop=(k == KT - 1))
                        ins.then_inc(tile_ready[n % 2], 1)
                    elif kind == "v":
                        g, t = x
                        c = chunk_of[kind, x]
                        pe.wait_ge(w_loaded[c % 2], 16 * (c // 2 + 1))
                        for k in range(KT):
                            ins = mm(ps[0:TOK[t], b, :], hT[:, k, tok(t)], W[:, c % 2, k, :], start=(k == 0),
                                     stop=(k == KT - 1))
                        ins.then_inc(tile_ready[n % 2], 1)
                    elif kind == "kT":
                        pe.wait_ge(kt_ready, x + 1)
                        if x:
                            pe.wait_ge(tails_ready, 1)
                        for h in range(GH):
                            b = empty(("kT", x, h))
                            for c in range(NC):
                                ins = tr(ps[:, b, c * P:c * P + P], Kl[:, h, c * P:c * P + P], ident[:, :])
                            ins.then_inc(bank_ready[b], 1)
                        b = empty(("kTs", x))
                        for h in range(GH):
                            ins = tr(ps[0:TS, b, h * P:h * P + P], Kl[:, h, TP:T], ident[:, :])
                        ins.then_inc(bank_ready[b], 1)
                    elif kind == "sc":
                        pe.wait_ge(lev_ready, 2 * (LEV * x[0] + x[1] + 1))
                        hs = 64 >> x[1]
                        for h in range(GH):
                            b = empty(("sc", x, h))
                            for c in range(NC):
                                ins = mm(ps[:, b, 64 * c:64 * c + 64], Kl[:, h, c * P:c * P + P], Ql[:, h, 64 * c:64 * c + 64],
                                         start=True, stop=True)
                            if hs <= 2:
                                ins = mm(ps[0:TS, b, 256:272], Kl[:, h, TP:T], Ql[:, h, 256:272], start=True, stop=True)
                            ins.then_inc(bank_ready[b], 1)
                    elif kind == "diag":
                        for h in range(GH):
                            b = empty(("diag", x, h))
                            for c in range(NC):
                                ins = mm(ps[:, b, P * c:P * c + P], X[:, h, c * P:c * P + P], Q[:, h, c * P:c * P + P],
                                         start=True, stop=True)
                            ins.then_inc(bank_ready[b], 1)
                        b = empty(("diags", x))
                        for h in range(GH):
                            ins = mm(ps[0:TS, b, h * TS:h * TS + TS], X[:, h, TP:T], Q[:, h, TP:T], start=True, stop=True)
                        ins.then_inc(bank_ready[b], 1)
                    elif kind == "stA":
                        g, h = x // 4, x % 4
                        if h == 0:
                            after_banks(pe, [("kT", g, i) for i in range(GH)] + [("kTs", g)])
                            for t in range(NT):
                                after_tile(pe, "v", (g, t))
                        b = empty(("inc", x))
                        for c in range(NC):
                            ins = mm(ps[:, b, c * P:c * P + P], ktT[:, h, c, :], V[:, c, h * P:h * P + P], start=True, stop=True)
                        ins.then_inc(bank_ready[b], 1)
                    elif kind == "stB":
                        g, h, s = x // 4, x % 4, x % 2
                        if h == 0:
                            after_banks(pe, [("diag", g, i) for i in range(GH)] + [("diags", g)])
                        after_banks(pe, [("inc", x)])
                        pe.wait_ge(vb_ready, x + 1)
                        b = empty(("o", x))
                        hv = slice(h * P, h * P + P)
                        for c in range(NC):
                            cc = slice(c * P, c * P + P)
                            ins = mm(ps[:, b, cc], V[:, c, hv], A[:, h, cc], start=True, stop=(c == 0))
                            if c:
                                ins = mm(ps[:, b, cc], S[:, c - 1, :], qc[:, h, cc], start=False, stop=True)
                        ins.then_inc(bank_ready[b], 1)
                        b = empty(("os", x))
                        pe.wait_ge(s0_loaded[s], 16 * (x // 2 + 1))
                        mm(ps[:, b, 0:TS], V[0:TS, 4, hv], A[0:TS, h, TP:T], start=True, stop=False)
                        for r in range(NB):
                            ins = mm(ps[:, b, r * TB:r * TB + TB], S0[:, s, r, :], qc[:, h, TP + r * TB:TP + r * TB + TB],
                                     start=False, stop=(r == NB - 1))
                        ins.then_inc(bank_ready[b], 1)
                        for i in range(2):
                            b = empty(("si", x, i))
                            mm(ps[:, b, :], ktTs[0:TS, h, :], Vb[0:TS, 4 * i:4 * i + 4, :].rearrange("p b d -> p (b d)"),
                               start=True, stop=True).then_inc(bank_ready[b], 1)
                    elif kind == "stat":
                        from_dve()
                        for s in range(2):
                            ins = mm(ps[:, b + s, 0:HF], ones[:, :], SG[:, x % 2, s * HF:s * HF + HF], start=True, stop=True)
                        ins.then_inc(tile_ready[n % 2], 1)
                    elif kind == "cvout":
                        from_dve()
                        after_banks(pe, [("si", 3, 0), ("os", 3)])
                        for k in range(KT):
                            ins = tr(ps[0:18, 6 + k // 4, (k % 4) * P:(k % 4) * P + P], ul[:, k, :], ident[:, :])
                        ins.then_inc(rows_ready, 1)

        x1_ready, r_ready, h2_ready = sem("x1_ready"), sem("rstd_ready"), sem("h2_ready")
        h2_out = [sem(f"h2_out{i}") for i in range(2)]
        wo_ready, h2t_ready, h2t_copied, lg_ready = sem("wo_ready"), sem("h2t_ready"), sem("h2t_copied"), sem("logits_ready")
        exp_asked, exp_done, m_ready, rank_ready = sem("exp_asked"), sem("exp_done"), sem("chosen_ready"), sem("rank_ready")
        rec_ready, rec_out, tab_in = sem("rec_ready"), sem("rec_out"), sem("table_loaded")
        step2 = {k: sem(f"{k}_step2") for k in ("act", "dve")}
        gu_loaded = [sem(f"gate_up_loaded{i}") for i in range(2)]
        dn_loaded = [sem(f"down_loaded{i}") for i in range(2)]
        xg_zero = sem("xg_zeroed")

        def load_expert(sp, e, s):
            gate = a["w_gate"][0][bass.ds(e, 1)].rearrange("e (k p) n -> p (e k) n", p=P)
            up = a["w_up"][0][bass.ds(e, 1)].rearrange("e (k p) n -> p (e k) n", p=P)
            sp.dma_start(wgu[s][:, :, 0:DE], gate).then_inc(gu_loaded[s], 16)
            sp.dma_start(wgu[s][:, :, DE:2 * DE], up).then_inc(gu_loaded[s], 16)

        def load_down(sp, e, s):
            down = a["w_down"][0][bass.ds(e, 1)].rearrange("e (k p) n -> p (e k) n", p=P)
            sp.dma_start(wdn[s][:, :, :], down).then_inc(dn_loaded[s], 16)

        with nc.Block() as block:

            @block.sync
            def _(sp):
                for s in range(2):
                    load_expert(sp, s, s)
                    load_down(sp, s, s)
                for t in range(NT):
                    sp.wait_ge(h2_ready, t + 1)
                    sp.dma_start(h2_dram[tok(t), :], h2[t % 2][0:TOK[t], :]).then_inc(h2_out[t % 2], 16)
                sp.wait_ge(rec_out, 16 * 2 * NT)
                sp.dma_start(tb, tab_dram.rearrange("(e r) c -> r e c", r=RANKS)[0:CAP]).then_inc(tab_in, 16)
                sp.wait_ge(h2_out[0], 48)
                sp.wait_ge(h2_out[1], 32)
                sp.wait_ge(tab_in, 16)
                sp.wait_ge(tab_set, 16)

            @block.gpsimd
            def _(pool):
                for i in range(2):
                    nc.gpsimd.memset(xg[i], 0.0).then_inc(xg_zero, 1)
                pool.wait_ge(xg_zero, 2)
                pool.wait_ge(tab_set, 16)
                for t in range(NT):
                    pool.wait_ge(rec_ready, t + 1)
                    for k in range(2):
                        n = TOK[t]
                        nc.gpsimd.indirect_dma_start(
                            out=tab_dram, out_offset=bass.IndirectOffsetOnAxis(ap=slot[0:n, t, k:k + 1], axis=0),
                            in_=rec[0:n, t, k, :], in_offset=None).then_inc(rec_out, 16)
                pool.wait_ge(rec_out, 16 * 2 * NT)

            @block.tensor
            def _(pe):
                mm, tr = nc.tensor.matmul, nc.tensor.transpose
                pe.wait_ge(r_loaded, 7 * 16)
                c0, c1 = wo_chunk, wo_chunk + 1
                for c in (c0, c1):
                    pe.wait_ge(w_loaded[c % 2], 16 * (c // 2 + 1))

                def project(t):
                    n, b = TOK[t], 2 * (t % 2)
                    if t >= 2:
                        pe.wait_ge(x1_ready, t - 1)
                    for k in range(KT):
                        for s, c in enumerate((c0, c1)):
                            ins = mm(ps[0:n, b + s, :], m[:, k, tok(t)], W[:, c % 2, k, :], start=(k == 0), stop=(k == KT - 1))
                    ins.then_inc(wo_ready, 1)

                project(0)
                project(1)
                for t in range(NT):
                    n = TOK[t]
                    pe.wait_ge(h2_ready, t + 1)
                    if t:
                        pe.wait_ge(h2t_copied, t)
                    for k in range(KT):
                        ins = tr(ps[:, 4 + k // 4, (k % 4) * P:(k % 4) * P + n], h2[t % 2][0:n, k * P:k * P + P], ident[0:n, 0:n])
                    ins.then_inc(h2t_ready, 1)
                    pe.wait_ge(h2t_copied, t + 1)
                    if t:
                        pe.wait_ge(exp_asked, t)
                    for k in range(KT):
                        ins = mm(ps[0:n, 6, 0:36], h2T[:, k, 0:n], wr[:, k, :], start=(k == 0), stop=(k == KT - 1))
                    ins.then_inc(lg_ready, 1)
                    if t + 2 < NT:
                        project(t + 2)
                    pe.wait_ge(m_ready, t + 1)
                    for u in range(t):
                        mm(ps[0:n, 7, 0:NE], ones[:, 0:n], M[:, u, :], start=(u == 0), stop=False)
                    mm(ps[0:n, 7, 0:NE], tri[0:n, 0:n], M[0:n, t, :], start=(t == 0), stop=True).then_inc(rank_ready, 1)
                for u in range(NT):
                    ins = mm(ps[:, 5, 0:NE], ones[0:TOK[u], :], M[0:TOK[u], u, :], start=(u == 0), stop=(u == NT - 1))
                ins.then_inc(rank_ready, 1)

            @block.scalar
            def _(act):
                step = Count()

                def link(ins):
                    ins.then_inc(step2["act"], 1)
                    act.wait_ge(step2["act"], step.next())

                def norm(t):
                    n = TOK[t]
                    act.wait_ge(x1_ready, t + 1)
                    if t >= 2:
                        act.wait_ge(h2_out[t % 2], 16 * (t // 2))
                        act.wait_ge(h2t_ready, t - 1)
                    link(nc.scalar.activation(h2[t % 2][0:n, :], x1[0:n, t, :], ACT.Square, accum_out=ss[0:n, t:t + 1]))
                    link(nc.scalar.activation(ss[0:n, t:t + 1], ss[0:n, t:t + 1], ACT.Ln, bias=eps[0:n, 0:1], scale=1.0 / D))
                    nc.scalar.activation(rs[0:n, t:t + 1], ss[0:n, t:t + 1], ACT.Exp, scale=-0.5).then_inc(r_ready, 1)

                norm(0)
                for t in range(NT):
                    n = TOK[t]
                    if t + 1 < NT:
                        norm(t + 1)
                    act.wait_ge(h2t_ready, t + 1)
                    if t:
                        act.wait_ge(lg_ready, t)
                    nc.scalar.activation(h2T[:, :, 0:n], ps[:, 4:6, :].rearrange("p s (k t) -> p (s k) t", k=4)[:, :, 0:n],
                                         ACT.Copy).then_inc(h2t_copied, 1)
                    act.wait_ge(exp_asked, t + 1)
                    link(nc.scalar.activation(g8[0:n, 4:8], lg[0:n, 0:4], ACT.Exp, bias=rf[0:n, 2:3], accum_out=rf[0:n, 0:1]))
                    nc.scalar.activation(rf[0:n, 1:2], top[0:n, 1, 1:2], ACT.Exp, bias=rf[0:n, 3:4]).then_inc(exp_done, 1)

            @block.vector
            def _(dve):
                v = nc.vector
                step = Count()

                def link(ins):
                    ins.then_inc(step2["dve"], 1)
                    dve.wait_ge(step2["dve"], step.next())

                dve.wait_ge(x1_loaded, NT * 16)
                dve.wait_ge(r_loaded, 7 * 16)
                link(v.memset(rec, 0))

                def residual(t):
                    n, b = TOK[t], 2 * (t % 2)
                    dve.wait_ge(wo_ready, t + 1)
                    y = x1[0:n, t, :].rearrange("p (s d) -> p s d", s=2)
                    v.tensor_tensor(y, y, ps[0:n, b:b + 2, :], ALU.add).then_inc(x1_ready, 1)

                residual(0)
                for t in range(NT):
                    n = TOK[t]
                    if t + 1 < NT:
                        residual(t + 1)
                    dve.wait_ge(r_ready, t + 1)
                    v.scalar_tensor_tensor(h2[t % 2][0:n, :], x1[0:n, t, :], rs[0:n, t:t + 1], gffn[0:n, :], ALU.mult,
                                           ALU.mult).then_inc(h2_ready, 1)
                    dve.wait_ge(lg_ready, t + 1)
                    L = lg[0:n, :]
                    link(v.tensor_tensor(L, ps[0:n, 6, 0:36], rb[0:n, :], ALU.add))
                    link(v.memset(g8[0:n, 4:8], -3.0e38))
                    link(v.tensor_copy(g8[0:n, 0:4], L[:, 0:4]))
                    link(v.max(top[0:n, 0, :], g8[0:n, :]))
                    link(v.max_index(topi[0:n, 0, :], top[0:n, 0, :], g8[0:n, :]))
                    link(v.tensor_scalar(rf[0:n, 2:3], top[0:n, 0, 0:1], -1.0, None, ALU.mult))
                    link(v.tensor_copy(rf[0:n, 4:5], topi[0:n, 0, 0:1]))
                    link(v.tensor_scalar(junk[0:n, 0:4], iota[0:n, 0:4], rf[0:n, 4:5], None, ALU.is_equal))
                    link(v.tensor_scalar(sel[0:n, :], L[:, 4:12], junk[0:n, 0:1], None, ALU.mult))
                    for g in range(1, NG):
                        link(v.scalar_tensor_tensor(sel[0:n, :], L[:, 4 + 8 * g:12 + 8 * g], junk[0:n, g:g + 1], sel[0:n, :],
                                                    ALU.mult, ALU.add))
                    link(v.max(top[0:n, 1, :], sel[0:n, :]))
                    link(v.max_index(topi[0:n, 1, :], top[0:n, 1, :], sel[0:n, :]))
                    v.tensor_scalar(rf[0:n, 3:4], top[0:n, 1, 0:1], -1.0, None, ALU.mult).then_inc(exp_asked, 1)
                    link(v.tensor_copy(rf[0:n, 5:7], topi[0:n, 1, 0:2]))
                    for k in range(2):
                        link(v.scalar_tensor_tensor(rf[0:n, 7 + k:8 + k], rf[0:n, 4:5], float(EG), rf[0:n, 5 + k:6 + k],
                                                    ALU.mult, ALU.add))
                        link(v.tensor_scalar(oh[0:n, k, :], iota[0:n, :], rf[0:n, 7 + k:8 + k], None, ALU.is_equal))
                    v.tensor_tensor(M[0:n, t, :], oh[0:n, 0, :], oh[0:n, 1, :], ALU.add).then_inc(m_ready, 1)
                    dve.wait_ge(exp_done, t + 1)
                    link(v.tensor_scalar(rf[0:n, 9:10], rf[0:n, 1:2], 1.0, rf[0:n, 0:1], ALU.add, ALU.mult))
                    link(v.reciprocal(rf[0:n, 11:12], rf[0:n, 9:10]))
                    link(v.tensor_tensor(rf[0:n, 12:13], rf[0:n, 11:12], rf[0:n, 1:2], ALU.mult))
                    dve.wait_ge(rank_ready, t + 1)
                    for k in range(2):
                        link(v.tensor_tensor(junk[0:n, :], oh[0:n, k, :], ps[0:n, 7, 0:NE], ALU.mult))
                        link(v.tensor_reduce(rf[0:n, 13 + k:14 + k], junk[0:n, :], AX.X, ALU.add))
                        link(v.scalar_tensor_tensor(slot[0:n, t, k:k + 1], rf[0:n, 7 + k:8 + k], float(RANKS),
                                                    rf[0:n, 13 + k:14 + k], ALU.mult, ALU.add))
                        link(v.tensor_copy(rec[0:n, t, k, 0:1], tokno[0:n, t:t + 1]))
                        link(v.tensor_scalar(rec[0:n, t, k, 1:2], tokno[0:n, t:t + 1], float(k * T), None, ALU.add))
                        link(v.tensor_copy(rec[0:n, t, k, 2:3].bitcast(F32), rf[0:n, 11 + k:12 + k]))
                    v.engine_nop().then_inc(rec_ready, 1)
                dve.wait_ge(rank_ready, NT + 1)
                link(v.tensor_reduce(rf[:, 15:16], ps[:, 5, 0:NE], AX.X, ALU.max))
                link(v.tensor_scalar(flag, rf[0:1, 15:16], float(CAP), None, ALU.is_gt))

        gathered = [sem(f"gathered{i}") for i in range(2)]
        g_idx, s_idx = sem("gather_index"), sem("scatter_index")
        t_ready, t_cp_a, t_cp_v = sem("xg_transposed"), sem("xgT_copied_act"), sem("xgT_copied_dve")
        gu_ready, tanh_done, hid_ready = sem("gate_up_ready"), sem("tanh_done"), sem("hid_ready")
        ht_ready, ht_copied, dn_ready = sem("hidT_ready"), sem("hidT_copied"), sem("down_ready")
        yo_a, yo_v = sem("rows_copied_act"), sem("rows_copied_dve")
        y_out = [sem(f"expert_rows_out{i}") for i in range(2)]
        vstep = sem("expert_dve_step")
        ple_w, p_loaded = sem("ple_gate_loaded"), sem("ple_loaded")

        with nc.Block() as block:

            @block.sync
            def _(sp):
                for c in range(2):
                    sp.dma_start(W[:, c], a["w_ple_gate"][0][:, 512 * c:512 * c + 512].rearrange("(k p) n -> p k n", p=P)).then_inc(ple_w, 16)
                sp.dma_start(wpp, a["w_ple_proj"][0].rearrange("(k p) n -> p k n", p=P)).then_inc(p_loaded, 16)
                sp.dma_start(pt[:, 0:4, :], a["p_prompt"][0, 0].rearrange("(n p) d -> p n d", p=P)).then_inc(p_loaded, 16)
                sp.dma_start(pt[0:TS, 4, :], a["p_sample"][0].rearrange("b t d -> (b t) d")).then_inc(p_loaded, 16)
                sp.wait_ge(gu_ready, 1)
                load_expert(sp, 2, 0)
                with sp.Fori(0, NE // 2 - 2) as i:
                    for s in range(2):
                        e = 2 * i + s + 1
                        sp.wait_ge(gu_ready, e + 1)
                        load_expert(sp, e + 2, 1 - s)
                        sp.wait_ge(dn_ready, e)
                        load_down(sp, e + 1, s)
                sp.wait_ge(gu_ready, NE - 2)
                load_expert(sp, NE - 1, 1)
                for e in (NE - 3, NE - 2):
                    sp.wait_ge(dn_ready, e)
                    load_down(sp, e + 1, (e + 1) % 2)
                sp.wait_ge(ple_w, 32)
                sp.wait_ge(p_loaded, 48)

            @block.gpsimd
            def _(pool):
                zero, bound = pool.to_reg(0), pool.alloc_register("bound")

                def gather(e, s, first=False):
                    if not first:
                        pool.wait_ge(t_ready, e - 1)
                    nc.gpsimd.tensor_copy(gidx[s], tb[:, bass.ds(e, 1), 0]).then_inc(g_idx, 1)
                    pool.wait_ge(g_idx, e + 1)
                    pool.reg_add(bound, zero, T - 1)
                    nc.gpsimd.indirect_dma_start(out=xg[s], out_offset=None, in_=h2_dram,
                                                 in_offset=bass.IndirectOffsetOnAxis(ap=gidx[s], axis=0),
                                                 bounds_check=bound, oob_is_err=False).then_inc(gathered[s], 16)

                def scatter(e, s):
                    pool.wait_ge(yo_a, e + 1)
                    pool.wait_ge(yo_v, e + 1)
                    nc.gpsimd.tensor_copy(sidx[s], tb[:, bass.ds(e, 1), 1]).then_inc(s_idx, 1)
                    pool.wait_ge(s_idx, e + 1)
                    pool.reg_add(bound, zero, 2 * T - 1)
                    nc.gpsimd.indirect_dma_start(out=y_dram, out_offset=bass.IndirectOffsetOnAxis(ap=sidx[s], axis=0),
                                                 in_=yo[s], in_offset=None,
                                                 bounds_check=bound, oob_is_err=False).then_inc(y_out[s], 16)

                gather(0, 0, True)
                gather(1, 1, True)
                gather(2, 0)
                with pool.Fori(0, NE // 2 - 2) as i:
                    for s in range(2):
                        gather(2 * i + s + 3, 1 - s)
                        scatter(2 * i + s, s)
                gather(NE - 1, 1)
                for e in range(NE - 4, NE):
                    scatter(e, e % 2)
                for s in range(2):
                    pool.wait_ge(y_out[s], 16 * (NE // 2))

            def wait_for(eng, sem, value):
                if not isinstance(value, int) or value > 0:
                    eng.wait_ge(sem, value)

            def phases(eng, prologue, body):
                prologue()
                for s in range(2):
                    body(s, s, True, True)
                with eng.Fori(1, NE // 2 - 1) as i:
                    for s in range(2):
                        body(2 * i + s, s, True, True)
                body(NE - 2, 0, True, False)
                body(NE - 1, 1, False, False)

            @block.tensor
            def _(pe):
                mm, tr = nc.tensor.matmul, nc.tensor.transpose

                def turn(e, s, n):
                    pe.wait_ge(gathered[s], n)
                    wait_for(pe, t_cp_a, e)
                    wait_for(pe, t_cp_v, e)
                    for k in range(KT):
                        ins = tr(ps[:, k // 4, (k % 4) * P:(k % 4) * P + P], xg[s][:, k * P:k * P + P], ident[:, :])
                    ins.then_inc(t_ready, 1)

                def gate_up(e, s, n):
                    pe.wait_ge(gu_loaded[s], n)
                    pe.wait_ge(t_cp_a, e + 1)
                    pe.wait_ge(t_cp_v, e + 1)
                    wait_for(pe, hid_ready, e - 1)
                    for k in range(KT):
                        ins = mm(ps[:, 2 + s, :], xgT[s][:, k, :], wgu[s][:, k, :], start=(k == 0), stop=(k == KT - 1))
                    ins.then_inc(gu_ready, 1)

                def body(e, s, more, more2):
                    half = (e - s) // 2 if isinstance(e, int) else None
                    i16 = lambda add: 16 * (half + add) if half is not None else 8 * (e - s) + 16 * add
                    pe.wait_ge(hid_ready, e + 1)
                    for k in range(2):
                        ins = tr(ps[:, 6, k * P:k * P + P], hid[s][:, k * P:k * P + P], ident[:, :])
                    ins.then_inc(ht_ready, 1)
                    if more:
                        n1 = 1 if s == 0 else 2
                        gate_up(e + 1, 1 - s, 2 * i16(n1))
                    if more2:
                        turn(e + 2, s, i16(2))
                    pe.wait_ge(dn_loaded[s], i16(1))
                    pe.wait_ge(ht_copied, e + 1)
                    wait_for(pe, yo_a, e)
                    wait_for(pe, yo_v, e)
                    for k in range(2):
                        for c in range(2):
                            ins = mm(ps[:, 4 + c, :], hidT[s][:, k, :], wdn[s][:, k, 512 * c:512 * c + 512], start=(k == 0),
                                     stop=(k == 1))
                    ins.then_inc(dn_ready, 1)

                def prologue():
                    turn(0, 0, 16)
                    turn(1, 1, 16)
                    gate_up(0, 0, 32)

                phases(pe, prologue, body)

            @block.scalar
            def _(act):
                def copy_t(e, s):
                    act.wait_ge(t_ready, e + 1)
                    wait_for(act, gu_ready, e - 1)
                    nc.scalar.activation(xgT[s][:, 0:4, :], ps[:, 0, :].rearrange("p (k t) -> p k t", k=4),
                                         ACT.Copy).then_inc(t_cp_a, 1)

                def gate(e, s):
                    act.wait_ge(gu_ready, e + 1)
                    wait_for(act, hid_ready, e - 1)
                    nc.scalar.activation(sg[s], ps[:, 2 + s, 0:DE], ACT.Tanh, scale=0.5).then_inc(tanh_done, 1)

                def rows_out(e, s, n):
                    act.wait_ge(dn_ready, e + 1)
                    wait_for(act, y_out[s], n)
                    nc.scalar.activation(yo[s][:, 0:512], ps[:, 4, :], ACT.Copy).then_inc(yo_a, 1)

                def body(e, s, more, more2):
                    if more:
                        gate(e + 1, 1 - s)
                    if more2:
                        copy_t(e + 2, s)
                    rows_out(e, s, 8 * (e - s))

                def prologue():
                    copy_t(0, 0)
                    copy_t(1, 1)
                    gate(0, 0)

                phases(act, prologue, body)

            @block.vector
            def _(dve):
                v = nc.vector

                def copy_t(e, s):
                    dve.wait_ge(t_ready, e + 1)
                    wait_for(dve, gu_ready, e - 1)
                    v.tensor_copy(xgT[s][:, 4:8, :], ps[:, 1, :].rearrange("p (k t) -> p k t", k=4)).then_inc(t_cp_v, 1)

                def gate(e, s):
                    dve.wait_ge(tanh_done, e + 1)
                    v.tensor_scalar(sg[s], sg[s], 0.5, 0.5, ALU.mult, ALU.add).then_inc(vstep, 1)
                    dve.wait_ge(vstep, 2 * e + 1)
                    v.tensor_tensor(sg[s], sg[s], ps[:, 2 + s, 0:DE], ALU.mult).then_inc(vstep, 1)
                    dve.wait_ge(vstep, 2 * e + 2)
                    wait_for(dve, ht_ready, e - 1)
                    v.scalar_tensor_tensor(hid[s], sg[s], tb[:, bass.ds(e, 1), 2].bitcast(F32),
                                           ps[:, 2 + s, DE:2 * DE], ALU.mult, ALU.mult).then_inc(hid_ready, 1)

                def rows_out(e, s, n):
                    dve.wait_ge(dn_ready, e + 1)
                    wait_for(dve, y_out[s], n)
                    v.tensor_copy(yo[s][:, 512:1024], ps[:, 5, :]).then_inc(yo_v, 1)

                def body(e, s, more, more2):
                    dve.wait_ge(ht_ready, e + 1)
                    wait_for(dve, dn_ready, e - 1)
                    v.tensor_copy(hidT[s], ps[:, 6, 0:DE].rearrange("p (k t) -> p k t", k=2)).then_inc(ht_copied, 1)
                    if more:
                        gate(e + 1, 1 - s)
                    if more2:
                        copy_t(e + 2, s)
                    rows_out(e, s, 8 * (e - s))

                def prologue():
                    copy_t(0, 0)
                    copy_t(1, 1)
                    gate(0, 0)

                phases(dve, prologue, body)

        over = nc.values_load(flag, min_val=0, max_val=1)
        f_w, f_tab, f_xg, f_y = (sem(n) for n in ("more_weights", "more_table", "more_gathered", "more_stored"))
        f_t, f_tc, f_gu, f_tanh, f_hid, f_ht, f_hc, f_dn, f_yo, f_v = (sem("more_" + n) for n in (
            "transposed", "copied", "gate_up", "tanh", "hid", "hidT", "hidT_copied", "down", "rows", "dve_step"))
        BLOCKS = (T - CAP + P - 1) // P

        with nc.If(over > 0):
            with nc.Block() as block:

                @block.sync
                def _(sp):
                    def blocks(e):
                        for b in range(BLOCKS):
                            if not (isinstance(e, int) and b == 0):
                                sp.wait_ge(f_y, 16 * BLOCKS * e + 16 * b)
                            if b == 0:
                                one = bass.ds(e, 1)
                                sp.dma_start(wgu[0][:, :, 0:DE], a["w_gate"][0][one].rearrange("e (k p) n -> p (e k) n", p=P)).then_inc(f_w, 16)
                                sp.dma_start(wgu[0][:, :, DE:2 * DE], a["w_up"][0][one].rearrange("e (k p) n -> p (e k) n", p=P)).then_inc(f_w, 16)
                                sp.dma_start(wdn[0], a["w_down"][0][one].rearrange("e (k p) n -> p (e k) n", p=P)).then_inc(f_w, 16)
                                sp.wait_ge(f_w, 48 * e + 48)
                            sp.dma_start(ftab, tab_dram[bass.ds(RANKS * e + P * b + CAP, P), :]).then_inc(f_tab, 16)

                    blocks(0)
                    with sp.Fori(1, NE) as e:
                        blocks(e)
                    sp.wait_ge(f_y, 16 * BLOCKS * NE)

                @block.gpsimd
                def _(pool):
                    zero, bound = pool.to_reg(0), pool.alloc_register("more_bound")
                    with pool.Fori(0, NE * BLOCKS) as j:
                        pool.wait_ge(f_tab, 16 * j + 16)
                        pool.reg_add(bound, zero, T - 1)
                        nc.gpsimd.indirect_dma_start(out=xg[0], out_offset=None, in_=h2_dram,
                                                     in_offset=bass.IndirectOffsetOnAxis(ap=ftab[:, 0:1], axis=0),
                                                     bounds_check=bound, oob_is_err=False).then_inc(f_xg, 16)
                        pool.wait_ge(f_yo, j + 1)
                        pool.reg_add(bound, zero, 2 * T - 1)
                        nc.gpsimd.indirect_dma_start(out=y_dram, out_offset=bass.IndirectOffsetOnAxis(ap=ftab[:, 1:2], axis=0),
                                                     in_=yo[0], in_offset=None, bounds_check=bound,
                                                     oob_is_err=False).then_inc(f_y, 16)

                @block.tensor
                def _(pe):
                    mm, tr = nc.tensor.matmul, nc.tensor.transpose
                    with pe.Fori(0, NE * BLOCKS) as j:
                        pe.wait_ge(f_xg, 16 * j + 16)
                        for k in range(KT):
                            ins = tr(ps[:, k // 4, (k % 4) * P:(k % 4) * P + P], xg[0][:, k * P:k * P + P], ident[:, :])
                        ins.then_inc(f_t, 1)
                        pe.wait_ge(f_tc, j + 1)
                        for k in range(KT):
                            ins = mm(ps[:, 2, :], xgT[0][:, k, :], wgu[0][:, k, :], start=(k == 0), stop=(k == KT - 1))
                        ins.then_inc(f_gu, 1)
                        pe.wait_ge(f_hid, j + 1)
                        for k in range(2):
                            ins = tr(ps[:, 6, k * P:k * P + P], hid[0][:, k * P:k * P + P], ident[:, :])
                        ins.then_inc(f_ht, 1)
                        pe.wait_ge(f_hc, j + 1)
                        for k in range(2):
                            for c in range(2):
                                ins = mm(ps[:, 4 + c, :], hidT[0][:, k, :], wdn[0][:, k, 512 * c:512 * c + 512],
                                         start=(k == 0), stop=(k == 1))
                        ins.then_inc(f_dn, 1)

                @block.scalar
                def _(act):
                    with act.Fori(0, NE * BLOCKS) as j:
                        act.wait_ge(f_gu, j + 1)
                        nc.scalar.activation(sg[0], ps[:, 2, 0:DE], ACT.Tanh, scale=0.5).then_inc(f_tanh, 1)

                @block.vector
                def _(dve):
                    v = nc.vector
                    with dve.Fori(0, NE * BLOCKS) as j:
                        dve.wait_ge(f_t, j + 1)
                        v.tensor_copy(xgT[0], ps[:, 0:2, :].rearrange("p s (k t) -> p (s k) t", k=4)).then_inc(f_tc, 1)
                        dve.wait_ge(f_tanh, j + 1)
                        v.tensor_scalar(sg[0], sg[0], 0.5, 0.5, ALU.mult, ALU.add).then_inc(f_v, 1)
                        dve.wait_ge(f_v, 2 * j + 1)
                        v.tensor_tensor(sg[0], sg[0], ps[:, 2, 0:DE], ALU.mult).then_inc(f_v, 1)
                        dve.wait_ge(f_v, 2 * j + 2)
                        v.scalar_tensor_tensor(hid[0], sg[0], ftab[:, 2:3].bitcast(F32), ps[:, 2, DE:2 * DE], ALU.mult,
                                               ALU.mult).then_inc(f_hid, 1)
                        dve.wait_ge(f_ht, j + 1)
                        v.tensor_copy(hidT[0], ps[:, 6, 0:DE].rearrange("p (k t) -> p k t", k=2)).then_inc(f_hc, 1)
                        dve.wait_ge(f_dn, j + 1)
                        v.tensor_copy(yo[0].rearrange("p (s d) -> p s d", s=2), ps[:, 4:6, :]).then_inc(f_yo, 1)

        y_in = [sem(f"expert_rows_in{t}") for t in range(NT)]
        x2_ready, r3_ready, h3_ready, h3t_ready, h3t_copied = (sem(n) for n in (
            "x2_ready", "rstd3_ready", "h3_ready", "h3t_ready", "h3t_copied"))
        pg_ready, pp_ready, tanh3, x3_ready, r4_ready, out_ready = (sem(n) for n in (
            "ple_gate_ready", "ple_proj_ready", "tanh3_done", "x3_ready", "rstd4_ready", "out_ready"))
        pt_ready, pt_copied = sem("pT_ready"), sem("pT_copied")
        y_stored = [sem(f"y_stored{i}") for i in range(2)]
        step3 = {k: sem(f"{k}_step3") for k in ("act", "dve")}

        with nc.Block() as block:

            @block.sync
            def _(sp):
                for t in range(NT):
                    for k in range(2):
                        r0 = k * T + t * P
                        sp.dma_start(yk[t][k][0:TOK[t], :], y_dram[r0:r0 + TOK[t], :]).then_inc(y_in[t], 16)
                for t in range(NT):
                    n = TOK[t]
                    sp.wait_ge(out_ready, t + 1)
                    dst = o["y_prompt"][0, t * P:t * P + P, :] if t < 4 else o["y_sample"].rearrange("b t d -> (b t) d")
                    sp.dma_start(dst, out3[t % 2][0:n, :]).then_inc(y_stored[t % 2], 16)
                sp.wait_ge(y_stored[0], 16 * 3)
                sp.wait_ge(y_stored[1], 16 * 2)

            @block.tensor
            def _(pe):
                mm, tr = nc.tensor.matmul, nc.tensor.transpose
                for t in range(NT):
                    n, b = TOK[t], 2 + 2 * (t % 2)
                    if t >= 2:
                        pe.wait_ge(pt_copied, t - 1)
                    for k in range(2):
                        ins = tr(ps[:, b + k, 0:n], pt[0:n, t, k * P:k * P + P], ident[0:n, 0:n])
                    ins.then_inc(pt_ready, 1)

                def turn(t):
                    n = TOK[t]
                    pe.wait_ge(h3_ready, t + 1)
                    if t:
                        pe.wait_ge(h3t_copied, t)
                    for k in range(KT):
                        ins = tr(ps[:, k // 4, (k % 4) * P:(k % 4) * P + n], h3[t % 2][0:n, k * P:k * P + P], ident[0:n, 0:n])
                    ins.then_inc(h3t_ready, 1)

                def ple_proj(t):
                    n = TOK[t]
                    if t:
                        pe.wait_ge(x3_ready, t)
                    for k in range(2):
                        for c in range(2):
                            ins = mm(ps[0:n, 4 + c, :], pT[:, k, tok(t)], wpp[:, k, 512 * c:512 * c + 512], start=(k == 0),
                                     stop=(k == 1))
                    ins.then_inc(pp_ready, 1)

                pe.wait_ge(pt_copied, NT)
                ple_proj(0)
                turn(0)
                for t in range(NT):
                    n, b = TOK[t], 2 + 4 * (t % 2)
                    if t >= 2:
                        pe.wait_ge(x3_ready, t - 1)
                    pe.wait_ge(h3t_copied, t + 1)
                    for k in range(KT):
                        for c in range(2):
                            ins = mm(ps[0:n, b + c, :], h3T[t % 2][:, k, 0:n], W[:, c, k, :], start=(k == 0), stop=(k == KT - 1))
                        if k == 0 and t == 0:
                            turn(1)
                    ins.then_inc(pg_ready, 1)
                    if t:
                        ple_proj(t)
                    if t + 2 < NT:
                        turn(t + 2)

            @block.scalar
            def _(act):
                step = Count()

                def link(ins):
                    ins.then_inc(step3["act"], 1)
                    act.wait_ge(step3["act"], step.next())

                def rms(t, sums, done):
                    n = TOK[t]
                    link(nc.scalar.activation(squares[0:n, :], x1[0:n, t, :], ACT.Square, accum_out=sums[0:n, t:t + 1]))
                    link(nc.scalar.activation(sums[0:n, t:t + 1], sums[0:n, t:t + 1], ACT.Ln, bias=eps[0:n, 0:1], scale=1.0 / D))
                    nc.scalar.activation(sums[0:n, t:t + 1], sums[0:n, t:t + 1], ACT.Exp, scale=-0.5).then_inc(done, 1)

                def norm2(t):
                    act.wait_ge(x2_ready, t + 1)
                    rms(t, rs, r3_ready)

                norm2(0)
                norm2(1)
                for t in range(NT):
                    n, b = TOK[t], 2 + 4 * (t % 2)
                    if t + 2 < NT:
                        norm2(t + 2)
                    act.wait_ge(pg_ready, t + 1)
                    if t >= 2:
                        act.wait_ge(x3_ready, t - 1)
                    nc.scalar.activation(s3[t % 2][0:n, :].rearrange("p (s d) -> p s d", s=2), ps[0:n, b:b + 2, :], ACT.Tanh,
                                         scale=0.5).then_inc(tanh3, 1)
                    act.wait_ge(x3_ready, t + 1)
                    rms(t, ss, r4_ready)

            @block.vector
            def _(dve):
                v = nc.vector
                step = Count()

                def link(ins):
                    ins.then_inc(step3["dve"], 1)
                    dve.wait_ge(step3["dve"], step.next())

                for t in range(NT):
                    n = TOK[t]
                    dve.wait_ge(pt_ready, t + 1)
                    b = 2 + 2 * (t % 2)
                    v.tensor_copy(pT[:, :, tok(t)], ps[:, b:b + 2, 0:n]).then_inc(pt_copied, 1)

                def experts_in(t):
                    n, x = TOK[t], x1[0:TOK[t], t, :]
                    dve.wait_ge(y_in[t], 32)
                    link(v.tensor_tensor(x, x, yk[t][0][0:n, :], ALU.add))
                    v.tensor_tensor(x, x, yk[t][1][0:n, :], ALU.add).then_inc(x2_ready, 1)
                    dve.wait_ge(r3_ready, t + 1)
                    if t >= 2:
                        dve.wait_ge(h3t_ready, t - 1)
                    v.tensor_scalar(h3[t % 2][0:n, :], x, rs[0:n, t:t + 1], None, ALU.mult).then_inc(h3_ready, 1)

                def turned(t):
                    n = TOK[t]
                    dve.wait_ge(h3t_ready, t + 1)
                    if t >= 2:
                        dve.wait_ge(pg_ready, t - 1)
                    v.tensor_tensor(h3T[t % 2][:, :, 0:n], ps[:, 0:2, :].rearrange("p s (k t) -> p (s k) t", k=4)[:, :, 0:n],
                                    gain[:, 16:24].unsqueeze(2).to_broadcast([P, 8, n]), ALU.mult).then_inc(h3t_copied, 1)

                experts_in(0)
                turned(0)
                experts_in(1)
                turned(1)
                for t in range(NT):
                    n, x = TOK[t], x1[0:TOK[t], t, :]
                    if t + 2 < NT:
                        experts_in(t + 2)
                    dve.wait_ge(tanh3, t + 1)
                    dve.wait_ge(pp_ready, t + 1)
                    s = s3[t % 2][0:n, :]
                    sv = s.rearrange("p (s d) -> p s d", s=2)
                    link(v.scalar_tensor_tensor(sv, sv, 1.0, ps[0:n, 4:6, :], ALU.add, ALU.mult))
                    v.scalar_tensor_tensor(x, s, 0.5, x, ALU.mult, ALU.add).then_inc(x3_ready, 1)
                    if t + 2 < NT:
                        turned(t + 2)
                    dve.wait_ge(r4_ready, t + 1)
                    if t >= 2:
                        dve.wait_ge(y_stored[t % 2], 16 * (t // 2))
                    v.scalar_tensor_tensor(out3[t % 2][0:n, :], x, ss[0:n, t:t + 1], gfin[0:n, :], ALU.mult, ALU.mult).then_inc(out_ready, 1)


_INS = ['x_prompt', 'x_sample', 'state_hgrn', 'state_conv', 'p_prompt', 'p_sample', 'g_mix', 'w_in', 'hg_lower',
        'g_hg_out', 'w_br_a', 'w_conv', 'w_br_b', 'w_out', 'g_ffn', 'w_router_group', 'b_router_group',
        'w_router_expert', 'b_router_expert', 'w_gate', 'w_up', 'w_down', 'g_ple', 'w_ple_gate', 'w_ple_proj',
        'g_final']
_OUTS = [("y_prompt", (1, TP, D)), ("y_sample", (NB, TB, D)), ("hgrn_prompt", (1, 1, NH, DK, DK)),
         ("conv_prompt", (1, 1, 2, D)), ("hgrn_sample", (1, NB, NH, DK, DK)), ("conv_sample", (1, NB, 2, D))]


def constants():
    s, t = np.arange(P)[:, None], np.arange(P)[None, :]
    lmask = np.zeros((P, LEV, 256), np.float32)
    smask = np.zeros((TS, 2, 16), np.float32)
    for l in range(LEV):
        hs = 64 >> l
        pair = (s // (2 * hs) == t // (2 * hs)) & (s % (2 * hs) < hs) & (t % (2 * hs) >= hs)
        late = pair[:, (np.arange(P) % (2 * hs)) >= hs]
        lmask[:, l] = np.tile(late, (1, NC))
        if hs <= 2:
            smask[:, l - 5] = late[0:TS, 0:16]
    small = np.zeros((P, 64), np.float32)
    small[:, 0:8] = (s // TB == np.arange(NB)[None, :])
    small[:, 8:40] = np.arange(NE)[None, :]
    small[:, 40:45] = s + P * np.arange(NT)[None, :]
    return dict(c_ident=np.eye(P, dtype=np.float32), c_tri=(s < t).astype(np.float32), c_lmask=lmask,
                c_smask=smask, c_small=small)


def kernel(**inputs):
    import concourse.bacc as _bacc
    from concourse.bass_utils import run_bass_kernel_spmd as _run

    nc = _bacc.Bacc("TRN2", target_bir_lowering=False, num_devices=1)
    arrays, ins, outs = {}, {}, {}
    for name in _INS:
        arrays[f"in_{name}"] = np.ascontiguousarray(inputs[name])
    for name, x in constants().items():
        arrays[f"in_{name}"] = x
    for name, x in arrays.items():
        ins[name[3:]] = nc.dram_tensor(name, x.shape, mybir.dt.from_np(x.dtype), kind="ExternalInput").ap()
    for name, shape in _OUTS:
        outs[name] = nc.dram_tensor(f"out_{name}", shape, F32, kind="ExternalOutput").ap()
    layer(nc, ins, outs)
    r = _run(nc, [arrays], core_ids=[0])
    return tuple(r.results[0][f"out_{name}"] for name, _ in _OUTS)
```

```python
from contextlib import ExitStack

import numpy as np

import concourse.bass as bass
from concourse import mybir

F32 = mybir.dt.float32
I32 = mybir.dt.int32
U32 = mybir.dt.uint32
U8 = mybir.dt.uint8
ALU = mybir.AluOpType
ACT = mybir.ActivationFunctionType
AX = mybir.AxisListType

P = 128
D = 1024
KT = D // P
TP = 512
NB, TB = 8, 4
TS = NB * TB
T = TP + TS
HF = T // 2
TOK = [128, 128, 128, 128, TS]
NT = len(TOK)
NH, DK = 8, 128
GH = 4
NC = TP // P
LEV = 7
NE, NG, EG = 32, 4, 8
DE = 256
PLE = 256
EPS = 1e-6
CAP = 64
RANKS = 640
UP = 64
FAR = 1 << 20
UW = 2 + TP + NB * (TB + 2)
COL = dict(q=0, fg=1024, v=2048, og=3072, cb=4096, cc=5120, ch=6144, ga=7168, gb=8192)

MIX = [("hT", KT * T), ("X", GH * T), ("cum", GH * T), ("Q", GH * T), ("V", NT * 512), ("Kl", GH * T),
       ("Ql", GH * HF), ("A", GH * T), ("qc", GH * T), ("ktT", 5 * 512), ("U", GH * UW), ("C", KT * T),
       ("oT", KT * T), ("m", KT * T), ("S", GH * P), ("S0", 2 * NB * P), ("Vb", NB * P), ("tmp", 2 * T)]


def schedule():
    ev = [("xT", t) for t in range(NT)]

    def tiles(kind, g):
        return [(kind, j) for j in (range(NT) if kind == "v" else range(4 * g, 4 * g + 4))]

    def front(g):
        return [*tiles("fg", g), ("gates", g), *tiles("q", g), ("qprep", g),
                *[("v", (g, t)) for t in range(NT)]]

    def attention(g):
        steps = [[("kT", g), ("lev", (g, 0))]]
        for l in range(LEV):
            steps.append([("sc", (g, l))] + ([("lev", (g, l + 1))] if l + 1 < LEV else []))
        steps.append([("diag", g)])
        for h in range(4 * g, 4 * g + 4):
            steps += [[("stA", h)], [("stB", h)]]
        return steps

    def weave(steps, fill, levels):
        out, n, done = [], 0, 0.0
        share = [levels if i <= LEV + 1 else 1.0 for i in range(len(steps))]
        size = [1.0 if kind in COL or kind in ("yb", "ya") else 0.15 for kind, _ in fill]
        for i, s in enumerate(steps):
            out += s
            done += share[i] / sum(share) * sum(size)
            while n < len(fill) and sum(size[:n + 1]) <= done + 0.01:
                out.append(fill[n])
                n += 1
        return out

    ev += front(0)
    ev += weave(attention(0), [x for g in range(2) for k in ("cc", "ch", "cb") for x in tiles(k, g)], 1.5)
    ev += [("cvout", 0)]
    ev += front(1)
    yb = tiles("yb", 1)
    ev += weave(attention(1), tiles("gb", 0) + tiles("yb", 0) + tiles("gb", 1) + yb[0:2] + [("stat", 0), ("stat", 1), yb[2],
                              ("norm", 1), ("stat", 2), ("stat", 3), yb[3], ("norm", 3)] + tiles("og", 0), 1.0)
    for j in (4, 6):
        ev += [("ga", j - 4), ("stat", j), ("stat", j + 1), ("ga", j - 3), ("norm", j + 1)]
    ev += tiles("og", 1)
    ev += [("pT", t) for t in range(NT)]
    ev += tiles("ya", 0) + tiles("ga", 1) + tiles("ya", 1)
    return ev + [("pp", 0), ("pp", 1)]


TILE_KINDS = {"xT", "fg", "q", "v", "cc", "ch", "cb", "stat", "og", "gb", "yb", "ga", "ya"}


class Count:

    def __init__(self, by=1):
        self.n, self.by = 0, by

    def next(self):
        self.n += self.by
        return self.n


def layer(nc, a, o):
    ev = schedule()

    chunks, chunk_of, last_tile = [], {}, {}
    tile_no, n = {}, 0
    for kind, x in ev:
        if kind not in TILE_KINDS:
            continue
        tile_no[kind, x] = n
        if kind not in ("xT", "stat"):
            g = x[0] if kind == "v" else x // 4
            if kind in ("yb", "ya"):
                key = (kind, g, a["w_br_b" if kind == "yb" else "w_br_a"][0][:, 512 * g:512 * g + 512])
            else:
                key = (kind, g, a["w_in"][0][:, COL[kind] + 512 * g:COL[kind] + 512 * g + 512])
            if not chunks or chunks[-1][:2] != key[:2]:
                chunks.append(key)
            chunk_of[kind, x] = len(chunks) - 1
            last_tile[len(chunks) - 1] = n
        n += 1
    for c in range(2):
        chunks.append(("wo", c, a["w_out"][0][:, 512 * c:512 * c + 512]))
    wo_chunk = len(chunks) - 2

    bank_use, used = {}, {b: 0 for b in (4, 5, 6, 7)}

    def use(key, b):
        bank_use[key] = (b, used[b])
        used[b] += 1

    for kind, x in ev:
        if kind == "kT":
            for h in range(GH):
                use(("kT", x, h), 4 + h)
            use(("kTs", x), 6)
        elif kind == "sc":
            for h in range(GH):
                use(("sc", x, h), 4 + h)
        elif kind == "diag":
            for h in range(GH):
                use(("diag", x, h), 4 + h)
            use(("diags", x), 6)
        elif kind == "stA":
            use(("inc", x), 4)
        elif kind == "stB":
            use(("o", x), 5)
            use(("os", x), 7)
            use(("si", x, 0), 6)
            use(("si", x, 1), 4)

    with ExitStack() as ctx:
        def sb(name, shape, dt=F32):
            return ctx.enter_context(nc.sbuf_tensor(name, shape, dt))

        def sem(name):
            return ctx.enter_context(nc.semaphore(name))

        W = sb("weights", [P, 2, KT, 512])
        arena = sb("arena", [P, sum(s for _, s in MIX)])
        R, at = {}, 0
        for name, size in MIX:
            R[name] = arena[:, at:at + size]
            R[name + "@"] = at
            at += size

        def area(off, size):
            return arena[:, off:off + size]

        hT = R["hT"].rearrange("p (k t) -> p k t", k=KT)
        X, cum, Q, A, qc, Kl = (R[k].rearrange("p (h t) -> p h t", h=GH) for k in ("X", "cum", "Q", "A", "qc", "Kl"))
        Ql = R["Ql"].rearrange("p (h t) -> p h t", h=GH)
        V = R["V"].rearrange("p (n d) -> p n d", n=NT)
        ktT = R["ktT"][:, 0:2048].rearrange("p (h c d) -> p h c d", h=GH, c=NC)
        ktTs = R["ktT"][:, 2048:2560].rearrange("p (h d) -> p h d", h=GH)
        U = R["U"].rearrange("p (j t) -> p j t", j=GH)
        squares1 = R["cum"].rearrange("p (j t) -> p j t", j=GH)
        SG = R["U"][:, 0:GH * T].rearrange("p (j t) -> p j t", j=GH)
        C, oT, m = (R[k].rearrange("p (k t) -> p k t", k=KT) for k in ("C", "oT", "m"))
        S = R["S"].rearrange("p (c d) -> p c d", c=NC)
        S0 = R["S0"].rearrange("p (s b d) -> p s b d", s=2, b=NB)
        Vb = R["Vb"].rearrange("p (b d) -> p b d", b=NB)
        tmp = R["tmp"].rearrange("p (s t) -> p s t", s=2)
        xt = area(R["C@"], NT * D).rearrange("p (n d) -> p n d", n=NT)
        cs = area(R["m@"], D)
        tab0 = area(R["m@"] + D, NE * RANKS * 4 // P).bitcast(I32)

        ident = sb("ident", [P, P])
        ones = sb("ones", [P, P])
        lmask = sb("level_masks", [P, LEV, 256], U8)
        smask = sb("sample_masks", [TS, 2, 16], U8)
        small = sb("small_consts", [P, 64])
        bmask, iota, tokno = small[:, 0:8], small[:, 8:40], small[:, 40:45]
        keep = sb("scan_keep", [P, TS])
        lmask_f = area(R["m@"] + 2 * D + P, LEV * 256)
        smask_f = area(R["m@"] + 2 * D + P + LEV * 256, 32)[0:TS]
        rows = area(R["m@"] + 2 * D, P)[0:48, :]
        gain = sb("gain_cols", [P, 48])
        cst = sb("conv_hist", [P, KT, 16])
        ul = sb("conv_tail", [P, KT, 18])
        ss = sb("sum_sq", [P, NT])
        rs = sb("rstd", [P, NT])
        nw = sb("newton", [P, NT])
        half_r = sb("half_rstd", [P, NT])
        El = sb("exp_last", [P, GH, NC + NB])
        eps = sb("eps", [P, 2])
        tails = area(R["tmp@"], D)

        ew = [area(i * 6144, 6144) for i in range(2)]
        wgu = [e[:, 0:4096].rearrange("p (k n) -> p k n", k=KT) for e in ew]
        wdn = [e[:, 4096:6144].rearrange("p (k n) -> p k n", k=2) for e in ew]
        at = R["V@"] + NT * 512
        x1 = area(at, NT * D).rearrange("p (n d) -> p n d", n=NT)
        at += NT * D
        h2_at = at
        h2 = [area(at + i * D, D) for i in range(2)]
        h2T = area(at + 2 * D, D).rearrange("p (k t) -> p k t", k=KT)
        at += 3 * D
        xg = [area(at + i * D, D) for i in range(2)]
        xgT = [area(at + (2 + i) * D, D).rearrange("p (k t) -> p k t", k=KT) for i in range(2)]
        moved = area(at + 2 * D, 512)
        h3T = [area(at + (2 + i) * D, D).rearrange("p (k t) -> p k t", k=KT) for i in range(2)]
        s3, out3 = [area(i * D, D) for i in range(2)], [area((2 + i) * D, D) for i in range(2)]
        squares = area(11 * D, D)
        assert 12 * D <= 2 * 6144
        at += 4 * D
        sg = [area(at + i * 256, 256) for i in range(2)]
        hid = [area(at + (2 + i) * 256, 256) for i in range(2)]
        hidT = [area(at + (4 + i) * 256, 256).rearrange("p (k t) -> p k t", k=2) for i in range(2)]
        at += 6 * 256
        yo = [area(at + i * D, D) for i in range(2)]
        at += 2 * D
        assert at <= R["oT@"]
        yk_at = [(4 + i) * D for i in range(7)] + [h2_at + i * D for i in range(3)]
        yk = [[area(yk_at[2 * t + k], D) for k in range(2)] for t in range(NT)]
        pt = area(R["C@"], NT * PLE).rearrange("p (n d) -> p n d", n=NT)
        pT = area(R["C@"] + NT * PLE, 2 * T).rearrange("p (k t) -> p k t", k=2)
        assert NT * PLE + 2 * T <= KT * T
        ppr = [area(R["oT@"] + t * D if t < 4 else R["m@"], D) for t in range(NT)]
        at = R["S@"]
        wpp = area(at, 2 * D).rearrange("p (k n) -> p k n", k=2)
        gffn = area(at + 2 * D, D)
        wr = area(at + 3 * D, KT * 36).rearrange("p (k n) -> p k n", k=KT)
        at += 3 * D + KT * 36
        assert at <= R["tmp@"]
        gfin = area(at, D)
        at += D
        M = area(at, NT * NE).rearrange("p (t e) -> p t e", t=NT)
        at += NT * NE
        tb = area(at, NE * 4).bitcast(I32).rearrange("p (e c) -> p e c", e=NE)
        at += NE * 4
        assert at <= R["tmp@"] + 2 * T
        at = R["hT@"] + 2 * 6144
        lg = area(at, 36)
        rb = area(at + 36, 36)
        g8, sel, rf = area(at + 72, 8), area(at + 80, 8), area(at + 88, 16)
        top = area(at + 104, 16).rearrange("p (k n) -> p k n", k=2)
        topi = area(at + 120, 16).bitcast(U32).rearrange("p (k n) -> p k n", k=2)
        oh = area(at + 136, 2 * NE).rearrange("p (k e) -> p k e", k=2)
        junk = area(at + 200, NE)
        slot = area(at + 232, 2 * NT).bitcast(I32).rearrange("p (t k) -> p t k", k=2)
        rec = area(at + 242, 8 * NT).bitcast(I32).rearrange("p (t k c) -> p t k c", t=NT, k=2)
        gidx = [area(at + 282 + i, 1).bitcast(I32) for i in range(2)]
        sidx = [area(at + 284 + i, 1).bitcast(I32) for i in range(2)]
        tri = area(at + 286, P)
        ftab = area(at + 414, 4).bitcast(I32)
        flag = area(at + 418, 1)[0:1].bitcast(I32)
        expj = area(at + 420, 4)
        own = area(at + 424, NG * EG).rearrange("p (g e) -> p g e", g=NG)
        before = area(at + 456, 2 * NE).rearrange("p (k e) -> p k e", k=2)
        up = [area(at + 456 + 2 * NE + i * DE, DE) for i in range(2)]
        assert at + 456 + 2 * NE + 2 * DE <= R["V@"] + NT * 512

        ps = ctx.enter_context(nc.psum_tensor("ps", [P, 8, 512], F32))

        h2_dram = nc.dram_tensor("h2_rows", [T, D], F32).ap()
        y_dram = nc.dram_tensor("expert_rows", [2 * T, D], F32).ap()
        tab_dram = nc.dram_tensor("route_table", [NE * RANKS, 4], I32).ap()

        tile_ready = [sem(f"tile_ready{p}") for p in range(2)]
        tile_freed = [sem(f"tile_freed{p}") for p in range(2)]
        bank_ready = {b: sem(f"bank_ready{b}") for b in used}
        bank_freed = {b: sem(f"bank_freed{b}") for b in used}
        w_loaded = [sem(f"w_loaded{s}") for s in range(2)]
        x_loaded = [sem(f"x_loaded{t}") for t in range(NT)]
        id_loaded, c_loaded, rows_loaded = sem("ident_loaded"), sem("consts_loaded"), sem("rows_loaded")
        rows_ready, rows_freed = sem("rows_ready"), sem("rows_freed")
        pool_set = sem("pool_set")
        act_step, dve_step, pool_step = sem("act_step"), sem("dve_step"), sem("pool_step")
        a2d, d2a = sem("act_to_dve"), sem("dve_to_act")
        d2p = sem("dve_to_pe")
        kt_ready, lev_ready, vb_ready = sem("kt_ready"), sem("lev_ready"), sem("vb_ready")
        a2p = sem("act_to_pe")
        p2d = sem("pool_to_dve")
        kl_zeroed = sem("kl_zeroed")
        s0_loaded = [sem(f"s0_loaded{i}") for i in range(2)]
        s0_out, s_out = [sem(f"s0_out{i}") for i in range(2)], sem("s_out")
        dve_state = sem("dve_state")
        x1_loaded, r_loaded = sem("x1_loaded"), sem("router_loaded")
        p_loaded, pt_ready, pt_copied, pp_ready = sem("ple_loaded"), sem("pT_ready"), sem("pT_copied"), sem("ple_proj_ready")
        pp_copied, gf_loaded = sem("ple_proj_copied"), sem("g_final_loaded")
        ple_w = sem("ple_gate_loaded")
        tab_ready, tab_set = sem("empty_table_ready"), sem("table_set")
        tails_ready, tails_out = sem("tails_ready"), sem("tails_out")

        def waits_tile(eng, kind, x):
            n = tile_no[kind, x]
            eng.wait_ge(tile_ready[n % 2], n // 2 + 1)
            return 2 * (n % 2), tile_freed[n % 2]

        def after_tile(eng, kind, x):
            n = tile_no[kind, x]
            eng.wait_ge(tile_freed[n % 2], n // 2 + 1)

        def full(eng, key):
            b, i = bank_use[key]
            eng.wait_ge(bank_ready[b], i + 1)
            return b, bank_freed[b]

        def after_banks(eng, keys):
            last = {}
            for key in keys:
                b, i = bank_use[key]
                last[b] = i + 1
            for b, i in last.items():
                eng.wait_ge(bank_freed[b], i)

        def rsqrt(v, link, x, y, u):
            link(v.tensor_scalar(y.bitcast(I32), x.bitcast(I32), -0.5, float(0x5F3759DF), ALU.mult, ALU.add))
            for _ in range(3):
                link(v.tensor_tensor(u, y, y, ALU.mult))
                link(v.tensor_tensor(u, u, x, ALU.mult))
                link(v.tensor_scalar(u, u, -0.5, 1.5, ALU.mult, ALU.add))
                link(v.tensor_tensor(y, y, u, ALU.mult))

        def rstd(v, link, sums, r):
            link(v.tensor_scalar(sums, sums, 1.0 / D, EPS, ALU.mult, ALU.add))
            rsqrt(v, link, sums, r, nw[0:r.shape[0], 0:r.shape[1]])

        def halves(b):
            return ps[:, b:b + 2, 0:HF]

        def split(x):
            return x.rearrange("p (s t) -> p s t", s=2)

        def tok(t):
            return slice(t * P, t * P + TOK[t])

        def lvl(x, l, heads=True):
            hs = 64 >> l
            if hs <= 2:
                return x.rearrange("p h (b two i) -> p (h b) two i", two=2, i=hs)
            return x[:, :, 0:TP].rearrange("p h (b two i) -> p h b two i", two=2, i=hs)

        def lvq(l):
            hs = 64 >> l
            if hs <= 2:
                return Ql.rearrange("p h (b i) -> p (h b) i", i=hs)
            return Ql[:, :, 0:256].rearrange("p h (b i) -> p h b i", i=hs)

        def at_half(t, c):
            u = UP * c if TOK[t] <= UP else 0
            return slice(u, u + TOK[t])

        def ple_proj(pe, t, b):
            for k in range(2):
                for c in range(2):
                    ins = nc.tensor.matmul(ps[at_half(t, c), b + c, :], pT[:, k, tok(t)], wpp[:, k, 512 * c:512 * c + 512],
                                           start=(k == 0), stop=(k == 1))
            ins.then_inc(pp_ready, 1)

        with nc.Block() as block:

            @block.sync
            def _(sp):
                sp.dma_start(ident[:, :], a["c_ident"]).then_inc(id_loaded, 16)
                for t in range(NT):
                    src = a["x_prompt"][0, t * P:t * P + P, :] if t < 4 else a["x_sample"].rearrange("b t d -> (b t) d")
                    sp.dma_start(xt[0:TOK[t], t, :], src).then_inc(x_loaded[t], 16)
                for i, (name, r0) in enumerate((("g_mix", 0), ("g_hg_out", 8), ("g_ple", 16))):
                    sp.dma_start(rows[r0:r0 + 8, :], a[name].rearrange("o (r p) -> (o r) p", p=P)).then_inc(rows_loaded, 16)
                sp.dma_start(rows[24:48, :], a["w_conv"].rearrange("o j (r p) -> (o j r) p", p=P)).then_inc(rows_loaded, 16)
                sp.dma_start(cs[0:16, :], a["state_conv"].rearrange("o b j c -> (o b j) c")).then_inc(rows_loaded, 16)
                n_chunk = [0]

                def load_chunk():
                    c = n_chunk[0]
                    n_chunk[0] += 1
                    if c >= 2:
                        last = last_tile[c - 2]
                        sp.wait_ge(tile_ready[last % 2], last // 2 + 1)
                    sp.dma_start(W[:, c % 2], chunks[c][2].rearrange("(k p) n -> p k n", p=P)).then_inc(w_loaded[c % 2], 16)

                load_chunk()
                sp.dma_start(small[:, :], a["c_small"]).then_inc(c_loaded, 16)
                sp.dma_start(lmask_f, a["c_lmask"].rearrange("p l t -> p (l t)")).then_inc(c_loaded, 16)
                sp.dma_start(smask_f, a["c_smask"].rearrange("p l t -> p (l t)")).then_inc(c_loaded, 16)
                load_chunk()
                sp.wait_ge(tab_ready, 1)
                sp.dma_start(tab_dram.rearrange("(p r) c -> p (r c)", p=P), tab0).then_inc(tab_set, 16)
                first_use = {c: min(i for i, e in enumerate(ev) if chunk_of.get(e) == c) for c in range(wo_chunk)}
                for i, (kind, x) in enumerate(ev):
                    if n_chunk[0] < len(chunks) and first_use.get(n_chunk[0] - 1, len(ev)) == i:
                        load_chunk()
                    if (kind, x) == ("ga", 0):
                        sp.wait_ge(s_out, 16 * NH)
                        sp.wait_ge(s0_out[0], 16 * 4)
                        sp.wait_ge(s0_out[1], 16 * 4)
                        sp.dma_start(pt[:, 0:4, :], a["p_prompt"][0, 0].rearrange("(n p) d -> p n d", p=P)).then_inc(p_loaded, 16)
                        sp.dma_start(pt[0:TS, 4, :], a["p_sample"][0].rearrange("b t d -> (b t) d")).then_inc(p_loaded, 16)
                        sp.dma_start(wpp, a["w_ple_proj"][0].rearrange("(k p) n -> p k n", p=P)).then_inc(p_loaded, 16)
                        for t in range(NT):
                            src = a["x_prompt"][0, t * P:t * P + P, :] if t < 4 else a["x_sample"].rearrange("b t d -> (b t) d")
                            sp.dma_start(x1[0:TOK[t], t, :], src).then_inc(x1_loaded, 16)
                        with nc.allow_non_contiguous_dma(reason="router weights"):
                            sp.dma_start(wr[:, :, 0:4], a["w_router_group"][0].rearrange("(k p) n -> p k n", p=P)).then_inc(r_loaded, 16)
                            sp.dma_start(wr[:, :, 4:36], a["w_router_expert"][0].rearrange("(k p) n -> p k n", p=P)).then_inc(r_loaded, 16)
                        sp.dma_start(rb[:, 0:4], a["b_router_group"].to_broadcast([P, 4])).then_inc(r_loaded, 16)
                        sp.dma_start(rb[:, 4:36], a["b_router_expert"].to_broadcast([P, 32])).then_inc(r_loaded, 16)
                        sp.dma_start(tri, a["c_tri"]).then_inc(r_loaded, 16)
                        sp.dma_start(gffn, a["g_ffn"].to_broadcast([P, D])).then_inc(r_loaded, 16)
                    if kind == "stA":
                        h, s = x, x % 2
                        if h >= 2:
                            sp.wait_ge(s0_out[s], 16 * (h // 2))
                        sp.dma_start(S0[:, s], a["state_hgrn"][0, :, h].rearrange("b k v -> k b v")).then_inc(s0_loaded[s], 16)
                    if kind == "stB":
                        h, s = x, x % 2
                        sp.wait_ge(dve_state, 2 * h + 1)
                        sp.dma_start(o["hgrn_prompt"][0, 0, h], S[:, NC - 1, :]).then_inc(s_out, 16)
                        sp.wait_ge(dve_state, 2 * h + 2)
                        sp.dma_start(o["hgrn_sample"][0, :, h].rearrange("b k v -> k b v"), S0[:, s]).then_inc(s0_out[s], 16)
                    if kind == "cvout":
                        sp.wait_ge(tails_ready, 1)
                        sp.dma_start(o["conv_prompt"][0, 0], tails[0:2, :]).then_inc(tails_out, 16)
                        sp.dma_start(o["conv_sample"][0].rearrange("b j c -> (b j) c"), tails[2:18, :]).then_inc(tails_out, 16)
                while n_chunk[0] < len(chunks):
                    load_chunk()
                sp.wait_ge(tails_out, 32)

            @block.gpsimd
            def _(pool):
                nc.gpsimd.memset(A, 0.0).then_inc(pool_set, 1)
                nc.gpsimd.memset(tab0, FAR).then_inc(pool_step, 1)
                pool.wait_ge(pool_step, 1)
                nc.gpsimd.memset(tab0.rearrange("p (r c) -> p r c", c=4)[:, :, 2:4], 0).then_inc(tab_ready, 1)
                for kind, x in ev:
                    if kind == "lev":
                        g, l = x
                        if l:
                            full(pool, ("sc", (g, l - 1), 3))
                        else:
                            for h in range(GH):
                                full(pool, ("kT", g, h))
                            full(pool, ("kTs", g))
                        v = lvl(Kl, l)
                        v = v[:, :, 1, :] if len(v.shape) == 4 else v[:, :, :, 1, :]
                        nc.gpsimd.memset(v, 0.0).then_inc(kl_zeroed, 1)

            @block.scalar
            def _(act):
                step, d2a_n = Count(), Count()

                def link(ins):
                    ins.then_inc(act_step, 1)
                    act.wait_ge(act_step, step.next())

                def from_dve():
                    act.wait_ge(d2a, d2a_n.next())

                from_dve()
                for kind, x in ev:
                    if kind == "xT":
                        n = TOK[x]
                        act.wait_ge(x_loaded[x], 16)
                        nc.scalar.activation(R["X"][0:n, 0:D], xt[0:n, x, :], ACT.Square, accum_out=ss[0:n, x:x + 1]).then_inc(a2d, 1)
                        act.wait_ge(a2d, x + 1)
                    elif kind == "fg":
                        b, freed = waits_tile(act, kind, x)
                        if x >= 4:
                            for h in range(GH):
                                full(act, ("diag", 0, h))
                            full(act, ("diags", 0))
                        nc.scalar.activation(split(X[:, x % 4, :]), halves(b), ACT.Copy).then_inc(freed, 1)
                    elif kind in ("q", "og"):
                        b, freed = waits_tile(act, kind, x)
                        from_dve()
                        nc.scalar.activation(split(tmp[:, x % 2, :]), halves(b), ACT.Tanh, scale=0.5).then_inc(a2d, 1)
                    elif kind == "v":
                        b, freed = waits_tile(act, kind, x)
                        g, t = x
                        if g:
                            for bank in (("o", 3), ("os", 3), ("si", 3, 0), ("si", 3, 1)):
                                full(act, bank)
                        if TOK[t] <= UP:
                            link(nc.scalar.activation(V[0:TOK[t], t, 0:256], ps[0:TOK[t], b, 0:256], ACT.Copy))
                            nc.scalar.activation(V[0:TOK[t], t, 256:512], ps[UP:UP + TOK[t], b, 0:256], ACT.Copy).then_inc(freed, 1)
                        else:
                            nc.scalar.activation(V[0:TOK[t], t, :], ps[0:TOK[t], b, :], ACT.Copy).then_inc(freed, 1)
                    elif kind == "gates":
                        from_dve()
                        link(nc.scalar.activation(qc, qc, ACT.Exp))
                        nc.scalar.activation(Kl, qc, ACT.Ln, bias=eps[:, 1:2]).then_inc(a2d, 1)
                        from_dve()
                        nc.scalar.activation(X, X, ACT.Exp).then_inc(a2d, 1)
                    elif kind == "qprep":
                        from_dve()
                        nc.scalar.activation(qc, cum, ACT.Exp).then_inc(a2d, 1)
                        nc.scalar.activation(El[:, :, 0:NC], cum[:, :, P - 1:TP:P], ACT.Exp).then_inc(a2d, 1)
                        nc.scalar.activation(El[:, :, NC:NC + NB], cum[:, :, TP + TB - 1:T:TB], ACT.Exp).then_inc(a2d, 1)
                        from_dve()
                        nc.scalar.activation(Kl, Kl, ACT.Exp).then_inc(a2d, 1)
                    elif kind == "kT":
                        for h in range(GH):
                            b, freed = full(act, ("kT", x, h))
                            nc.scalar.activation(ktT[:, h], ps[:, b, :].rearrange("p (c d) -> p c d", c=NC),
                                                 ACT.Copy).then_inc(freed, 1)
                        b, freed = full(act, ("kTs", x))
                        nc.scalar.activation(ktTs[0:TS], ps[0:TS, b, :].rearrange("p (h d) -> p h d", h=GH),
                                             ACT.Copy).then_inc(freed, 1)
                    elif kind == "lev":
                        g, l = x
                        from_dve()
                        q = lvq(l)
                        nc.scalar.activation(q, q, ACT.Exp).then_inc(a2d, 1)
                        from_dve()
                        k = lvl(Kl, l)
                        k = k[:, :, 0, :] if len(k.shape) == 4 else k[:, :, :, 0, :]
                        nc.scalar.activation(k, k, ACT.Exp).then_inc(a2d, 1)
                    elif kind == "stB":
                        b, freed = full(act, ("o", x))
                        nc.scalar.activation(oT[:, x, 0:TP], ps[:, b, :], ACT.Copy).then_inc(freed, 1)
                        b, freed = full(act, ("os", x))
                        nc.scalar.activation(oT[:, x, TP:T], ps[:, b, 0:TS], ACT.Copy).then_inc(freed, 1)
                    elif kind == "cc":
                        b, freed = waits_tile(act, kind, x)
                        nc.scalar.activation(split(C[:, x, :]), halves(b), ACT.Copy).then_inc(freed, 1)
                    elif kind == "ch":
                        j = x % 4
                        u = U[:, j, :]
                        from_dve()
                        nc.scalar.activation(u[:, 2:2 + TP], C[:, x, 0:TP], ACT.Copy).then_inc(a2d, 1)
                        us = u[:, 2 + TP:UW].rearrange("p (b t) -> p b t", b=NB)
                        nc.scalar.activation(us[:, :, 2:2 + TB], C[:, x, TP:T].rearrange("p (b t) -> p b t", b=NB),
                                             ACT.Copy).then_inc(a2d, 1)
                        nc.scalar.activation(us[:, :, 0:2], cst[:, x, :].rearrange("p (b t) -> p b t", b=NB),
                                             ACT.Copy).then_inc(a2d, 1)
                        nc.scalar.activation(ul[:, x, 0:2], C[:, x, TP - 2:TP], ACT.Copy).then_inc(a2d, 1)
                        nc.scalar.activation(ul[:, x, 2:18].rearrange("p (b t) -> p b t", b=NB),
                                             C[:, x, TP:T].rearrange("p (b t) -> p b t", b=NB)[:, :, 2:4],
                                             ACT.Copy).then_inc(a2d, 1)
                    elif kind == "stat":
                        if x % 2:
                            from_dve()
                            for j in (x - 1, x):
                                b, freed = waits_tile(act, kind, j)
                                nc.scalar.activation(split(tmp[:, j % 2, :]), halves(b), ACT.Ln, bias=eps[:, 0:1],
                                                     scale=1.0 / P).then_inc(freed, 1)
                    elif kind == "norm":
                        for j in (x - 1, x):
                            after_tile(act, "stat", j)
                            nc.scalar.activation(tmp[:, j % 2, :], tmp[:, j % 2, :], ACT.Exp, scale=-0.5).then_inc(a2d, 1)
                    elif kind in ("gb", "ga"):
                        b, freed = waits_tile(act, kind, x)
                        from_dve()
                        nc.scalar.activation(split(SG[:, x % 4, :]), halves(b), ACT.Tanh, scale=0.5).then_inc(freed, 1)
                    elif kind == "pT":
                        act.wait_ge(pt_ready, x + 1)
                        nc.scalar.activation(pT[:, :, tok(x)], ps[:, 4 + x % 4, 0:2 * P].rearrange("p (k t) -> p k t", k=2)[:, :, 0:TOK[x]],
                                             ACT.Copy).then_inc(pt_copied, 1)

            @block.vector
            def _(dve):
                v = nc.vector
                step, a2d_n = Count(), Count()

                def link(ins):
                    ins.then_inc(dve_step, 1)
                    dve.wait_ge(dve_step, step.next())

                def from_act():
                    dve.wait_ge(a2d, a2d_n.next())

                def sigmoid(x):
                    return v.tensor_scalar(x, x, 0.5, 0.5, ALU.mult, ALU.add)

                link(v.memset(ss[:, :], 0.0))
                link(v.memset(eps[:, 0:1], EPS))
                link(v.memset(eps[:, 1:2], 1.0))
                link(v.memset(keep[:, :], 1.0))
                link(v.memset(keep[:, 0:TS:TB], 0.0))
                v.memset(ones[:, :], 1.0).then_inc(d2a, 1)
                dve.wait_ge(d2a, 1)
                dve.wait_ge(pool_set, 1)
                dve.wait_ge(id_loaded, 16)

                def scaled(t):
                    n = TOK[t]
                    v.tensor_scalar(xt[0:n, t, :], xt[0:n, t, :], rs[0:n, t:t + 1], None, ALU.mult).then_inc(d2p, 1)

                for kind, x in ev:
                    if kind == "xT":
                        n = TOK[x]
                        if x == 0:
                            for t in range(NT):
                                from_act()
                                dve.wait_ge(x_loaded[t], 16)
                            rstd(v, link, ss[:, :], rs[:, :])
                            scaled(0)
                        if x + 1 < NT:
                            scaled(x + 1)
                        if x == 0:
                            dve.wait_ge(rows_ready, 1)
                            v.tensor_copy(gain[:, :], ps[:, 4, 0:48]).then_inc(rows_freed, 1)
                            dve.wait_ge(rows_ready, 2)
                            v.tensor_copy(cst[:, :, :], ps[:, 5, 0:128].rearrange("p (k c) -> p k c", k=KT)).then_inc(rows_freed, 1)
                            dve.wait_ge(rows_freed, 2)
                        b, freed = waits_tile(dve, kind, x)
                        v.tensor_tensor(hT[:, :, tok(x)],
                                        ps[:, b:b + 2, :].rearrange("p s (k t) -> p (s k) t", k=4)[:, :, 0:n],
                                        gain[:, 0:8].unsqueeze(2).to_broadcast([P, 8, n]), ALU.mult).then_inc(freed, 1)
                    elif kind == "gates":
                        if x == 0:
                            dve.wait_ge(c_loaded, 48)
                            link(v.tensor_copy(lmask[:, :, :].rearrange("p l t -> p (l t)"), lmask_f))
                            link(v.tensor_copy(smask[:, :, :].rearrange("p l t -> p (l t)"), smask_f))
                        for h in range(GH):
                            after_tile(dve, "fg", 4 * x + h)
                        if x:
                            full(dve, ("o", 3)), full(dve, ("os", 3))
                        v.scalar_tensor_tensor(R["qc"], R["X"], -1.0, R["X"], ALU.mult, ALU.min).then_inc(d2a, 1)
                        from_act()
                        link(v.scalar_tensor_tensor(R["qc"], R["X"], 0.0, R["Kl"], ALU.min, ALU.subtract))
                        v.tensor_tensor(X, qc, X, ALU.subtract).then_inc(d2a, 1)
                        for h in range(GH):
                            for c in range(NC):
                                s = slice(c * P, c * P + P)
                                v.tensor_tensor_scan(cum[:, h, s], ones[:, :], qc[:, h, s], 0.0, ALU.mult,
                                                     ALU.add).then_inc(dve_step, 1)
                                step.next()
                            v.tensor_tensor_scan(cum[:, h, TP:T], keep[:, :], qc[:, h, TP:T], 0.0, ALU.mult,
                                                 ALU.add).then_inc(dve_step, 1)
                            step.next()
                        from_act()
                    elif kind in ("q", "og"):
                        b, freed = waits_tile(dve, kind, x)
                        v.engine_nop().then_inc(d2a, 1)
                        from_act()
                        link(sigmoid(tmp[:, x % 2, :]))
                        if kind == "q":
                            v.tensor_tensor(split(Q[:, x % 4, :]), split(tmp[:, x % 2, :]), halves(b), ALU.mult).then_inc(freed, 1)
                            after_tile(dve, kind, x)
                        else:
                            link(v.tensor_tensor(split(tmp[:, x % 2, :]), split(tmp[:, x % 2, :]), halves(b), ALU.mult))
                            v.tensor_tensor(oT[:, x, :], oT[:, x, :], tmp[:, x % 2, :], ALU.mult).then_inc(freed, 1)
                            after_tile(dve, kind, x)
                    elif kind == "qprep":
                        dve.wait_ge(dve_step, step.n)
                        v.engine_nop().then_inc(d2a, 1)
                        last = cum[:, :, P - 1:TP:P]
                        link(v.tensor_tensor(Kl[:, :, 0:TP].rearrange("p h (c s) -> p h c s", s=P),
                                             last.unsqueeze(3).to_broadcast([P, GH, NC, P]),
                                             cum[:, :, 0:TP].rearrange("p h (c s) -> p h c s", s=P), ALU.subtract))
                        last = cum[:, :, TP + TB - 1:T:TB]
                        v.tensor_tensor(Kl[:, :, TP:T].rearrange("p h (c s) -> p h c s", s=TB),
                                        last.unsqueeze(3).to_broadcast([P, GH, NB, TB]),
                                        cum[:, :, TP:T].rearrange("p h (c s) -> p h c s", s=TB),
                                        ALU.subtract).then_inc(d2a, 1)
                        from_act()
                        link(v.tensor_tensor(qc, qc, Q, ALU.mult))
                        from_act(), from_act(), from_act()
                        v.tensor_tensor(Kl, Kl, X, ALU.mult).then_inc(kt_ready, 1)
                    elif kind == "lev":
                        g, l = x
                        hs = 64 >> l
                        if l:
                            full(dve, ("sc", (g, l - 1), 3))
                        else:
                            for h in range(GH):
                                full(dve, ("kT", g, h))
                            full(dve, ("kTs", g))
                        c4, k4, x4, q4, Q4 = lvl(cum, l), lvl(Kl, l), lvl(X, l), lvq(l), lvl(Q, l)
                        one, two = ((lambda y: y[:, :, 0, :]), (lambda y: y[:, :, 1, :])) if hs <= 2 else \
                            ((lambda y: y[:, :, :, 0, :]), (lambda y: y[:, :, :, 1, :]))
                        mid = one(c4)[..., hs - 1:hs].to_broadcast(list(one(c4).shape))
                        v.tensor_tensor(q4, two(c4), mid, ALU.subtract).then_inc(d2a, 1)
                        dve.wait_ge(kl_zeroed, LEV * g + l + 1)
                        v.tensor_tensor(one(k4), mid, one(c4), ALU.subtract).then_inc(d2a, 1)
                        from_act()
                        v.tensor_tensor(q4, q4, two(Q4), ALU.mult).then_inc(lev_ready, 1)
                        from_act()
                        v.tensor_tensor(one(k4), one(k4), one(x4), ALU.mult).then_inc(lev_ready, 1)
                    elif kind == "sc":
                        g, l = x
                        hs = 64 >> l
                        for h in range(GH):
                            if l == 0 and h == 0 and g:
                                full(dve, ("o", 3)), full(dve, ("os", 3))
                            b, freed = full(dve, ("sc", x, h))
                            dst = A[:, h, 0:TP].rearrange("p (b two i) -> p b two i", two=2, i=hs)[:, :, 1, :]
                            ins = v.copy_predicated(dst, lmask[:, l, :].rearrange("p (b i) -> p b i", i=hs),
                                                    ps[:, b, 0:256].rearrange("p (b i) -> p b i", i=hs))
                            if hs <= 2:
                                link(ins)
                                dst = A[0:TS, h, TP:T].rearrange("p (b two i) -> p b two i", two=2, i=hs)[:, :, 1, :]
                                ins = v.copy_predicated(dst, smask[:, l - 5, :].rearrange("p (b i) -> p b i", i=hs),
                                                        ps[0:TS, b, 256:272].rearrange("p (b i) -> p b i", i=hs))
                            ins.then_inc(freed, 1)
                        after_banks(dve, [("sc", x, h) for h in range(GH)])
                    elif kind == "diag":
                        for h in range(GH):
                            b, freed = full(dve, ("diag", x, h))
                            v.copy_predicated(A[:, h, 0:TP].rearrange("p (c t) -> p c t", c=NC),
                                              ident[:, :].bitcast(U32).unsqueeze(1).to_broadcast([P, NC, P]),
                                              ps[:, b, :].rearrange("p (c t) -> p c t", c=NC)).then_inc(freed, 1)
                        b, freed = full(dve, ("diags", x))
                        v.copy_predicated(A[0:TS, :, TP:T],
                                          ident[0:TS, 0:TS].bitcast(U32).unsqueeze(1).to_broadcast([TS, GH, TS]),
                                          ps[0:TS, b, 0:GH * TS].rearrange("p (h t) -> p h t", h=GH)).then_inc(freed, 1)
                    elif kind == "stA":
                        h = x % 4
                        if x:
                            full(dve, ("o", x - 1))
                            dve.wait_ge(s_out, 16 * x)
                            for i in range(2):
                                full(dve, ("si", x - 1, i))
                        b, freed = full(dve, ("inc", x))
                        link(v.tensor_copy(S[:, 0, :], ps[:, b, 0:P]))
                        for c in range(1, NC):
                            ins = v.scalar_tensor_tensor(S[:, c, :], S[:, c - 1, :], El[:, h, c:c + 1],
                                                         ps[:, b, c * P:c * P + P], ALU.mult, ALU.add)
                            if c < NC - 1:
                                link(ins)
                        ins.then_inc(freed, 1)
                        v.tensor_tensor(Vb[0:TS], V[0:TS, 4, h * P:h * P + P].unsqueeze(1).to_broadcast([TS, NB, P]),
                                        bmask[0:TS, :].unsqueeze(2).to_broadcast([TS, NB, P]), ALU.mult).then_inc(vb_ready, 1)
                        b, i = bank_use["inc", x]
                        dve.wait_ge(bank_freed[b], i + 1)
                        v.engine_nop().then_inc(dve_state, 1)
                    elif kind == "stB":
                        h, s = x % 4, x % 2
                        full(dve, ("os", x))
                        dec = El[:, h, NC:NC + NB].unsqueeze(2).to_broadcast([P, NB, P])
                        link(v.tensor_tensor(S0[:, s], S0[:, s], dec, ALU.mult))
                        for i in range(2):
                            b, freed = full(dve, ("si", x, i))
                            y = S0[:, s, 4 * i:4 * i + 4, :]
                            v.tensor_tensor(y, y, ps[:, b, :].rearrange("p (b d) -> p b d", b=4), ALU.add).then_inc(freed, 1)
                        after_banks(dve, [("si", x, 0), ("si", x, 1)])
                        v.engine_nop().then_inc(dve_state, 1)
                    elif kind == "ch":
                        b, freed = waits_tile(dve, kind, x)
                        after_tile(dve, "cc", x)
                        j = x % 4
                        u = U[:, j, :]
                        us = u[:, 2 + TP:UW].rearrange("p (b t) -> p b t", b=NB)
                        v.tensor_tensor(split(C[:, x, :]), split(C[:, x, :]), halves(b), ALU.mult).then_inc(freed, 1)
                        after_tile(dve, kind, x)
                        link(v.memset(u[:, 0:2], 0.0))
                        v.engine_nop().then_inc(d2a, 1)
                        for _ in range(5):
                            from_act()
                        cv = C[:, x, 0:TP]
                        cvs = C[:, x, TP:T].rearrange("p (b t) -> p b t", b=NB)
                        w = [gain[:, 24 + 8 * i + x:25 + 8 * i + x] for i in range(3)]
                        link(v.tensor_scalar(cv, u[:, 0:TP], w[0], None, ALU.mult))
                        link(v.tensor_scalar(cvs, us[:, :, 0:TB], w[0], None, ALU.mult))
                        for i in (1, 2):
                            link(v.scalar_tensor_tensor(cv, u[:, i:i + TP], w[i], cv, ALU.mult, ALU.add))
                            link(v.scalar_tensor_tensor(cvs, us[:, :, i:i + TB], w[i], cvs, ALU.mult, ALU.add))
                    elif kind == "cb":
                        b, freed = waits_tile(dve, kind, x)
                        v.tensor_tensor(split(C[:, x, :]), split(C[:, x, :]), halves(b), ALU.mult).then_inc(freed, 1)
                    elif kind == "cvout":
                        after_tile(dve, "cb", 6), after_tile(dve, "cb", 7)
                        v.engine_nop().then_inc(d2p, 1)
                        dve.wait_ge(rows_ready, 3)
                        link(v.tensor_copy(tails[0:18, 0:512], ps[0:18, 6, :]))
                        v.tensor_copy(tails[0:18, 512:1024], ps[0:18, 7, :]).then_inc(tails_ready, 1)
                        dve.wait_ge(tails_ready, 1)
                        dve.wait_ge(tails_out, 32)
                    elif kind == "stat":
                        b5, b7 = bank_use["o", x], bank_use["os", x]
                        dve.wait_ge(bank_freed[5], b5[1] + 1), dve.wait_ge(bank_freed[7], b7[1] + 1)
                        if x % 4 >= 2:
                            after_tile(dve, "stat", x - 2)
                        sq = SG if x < 4 else squares1
                        v.tensor_tensor(sq[:, x % 2, :], oT[:, x, :], oT[:, x, :], ALU.mult).then_inc(d2p, 1)
                        if x % 2:
                            v.engine_nop().then_inc(d2a, 1)
                    elif kind == "norm":
                        for j in (x - 1, x):
                            after_tile(dve, "stat", j)
                            from_act()
                            link(v.scalar_tensor_tensor(oT[:, j, :], oT[:, j, :], gain[:, 8 + j:9 + j], tmp[:, j % 2, :],
                                                        ALU.mult, ALU.mult))
                    elif kind in ("gb", "ga"):
                        v.engine_nop().then_inc(d2a, 1)
                        after_tile(dve, kind, x)
                        link(sigmoid(SG[:, x % 4, :]))
                    elif kind == "yb":
                        b, freed = waits_tile(dve, kind, x)
                        v.tensor_tensor(split(m[:, x, :]), split(SG[:, x % 4, :]), halves(b), ALU.mult).then_inc(freed, 1)
                        after_tile(dve, kind, x)
                    elif kind == "ya":
                        b, freed = waits_tile(dve, kind, x)
                        link(v.tensor_tensor(split(SG[:, x % 4, :]), split(SG[:, x % 4, :]), halves(b), ALU.mult))
                        v.tensor_tensor(m[:, x, :], m[:, x, :], SG[:, x % 4, :], ALU.add).then_inc(freed, 1)
                        after_tile(dve, kind, x)

            @block.tensor
            def _(pe):
                mm, tr = nc.tensor.matmul, nc.tensor.transpose
                d2p_n = Count()

                def from_dve():
                    pe.wait_ge(d2p, d2p_n.next())

                def empty(key):
                    b, i = bank_use[key]
                    if i:
                        pe.wait_ge(bank_freed[b], i)
                    return b

                pe.wait_ge(id_loaded, 16)
                pe.wait_ge(rows_loaded, 80)
                tr(ps[:, 4, 0:48], rows[:, :], ident[0:48, 0:48]).then_inc(rows_ready, 1)
                for k in range(KT):
                    ins = tr(ps[:, 5, 16 * k:16 * k + 16], cs[0:16, k * P:k * P + P], ident[0:16, 0:16])
                ins.then_inc(rows_ready, 1)
                pe.wait_ge(rows_freed, 2)
                tails_seen = False
                for kind, x in ev:
                    if kind in TILE_KINDS:
                        n = tile_no[kind, x]
                        b = 2 * (n % 2)
                        if n >= 2:
                            pe.wait_ge(tile_freed[n % 2], n // 2)
                    if kind == "xT":
                        r = TOK[x]
                        from_dve()
                        for k in range(KT):
                            ins = tr(ps[:, b + k // 4, (k % 4) * P:(k % 4) * P + r], xt[0:r, x, k * P:k * P + P],
                                     ident[0:r, 0:r])
                        ins.then_inc(tile_ready[n % 2], 1)
                    elif kind in COL and kind != "v" or kind in ("yb", "ya"):
                        if (kind, x) == ("fg", 0):
                            for t in range(NT):
                                after_tile(pe, "xT", t)
                        if (kind, x) == ("yb", 0):
                            for j in range(KT):
                                after_tile(pe, "cb", j)
                        if (kind, x) == ("ya", 0):
                            for j in range(KT):
                                after_tile(pe, "og", j)
                        c = chunk_of[kind, x]
                        pe.wait_ge(w_loaded[c % 2], 16 * (c // 2 + 1))
                        src = {"yb": C, "ya": oT}.get(kind, hT)
                        col = (x % 4) * P
                        for k in range(KT):
                            for s in range(2):
                                ins = mm(ps[:, b + s, 0:HF], W[:, c % 2, k, col:col + P], src[:, k, s * HF:s * HF + HF],
                                         start=(k == 0), stop=(k == KT - 1))
                        ins.then_inc(tile_ready[n % 2], 1)
                    elif kind == "v":
                        g, t = x
                        c = chunk_of[kind, x]
                        pe.wait_ge(w_loaded[c % 2], 16 * (c // 2 + 1))
                        for k in range(KT):
                            if TOK[t] <= UP:
                                for u in range(2):
                                    ins = mm(ps[u * UP:u * UP + TOK[t], b, 0:256], hT[:, k, tok(t)],
                                             W[:, c % 2, k, 256 * u:256 * u + 256], start=(k == 0), stop=(k == KT - 1))
                            else:
                                ins = mm(ps[0:TOK[t], b, :], hT[:, k, tok(t)], W[:, c % 2, k, :], start=(k == 0),
                                         stop=(k == KT - 1))
                        ins.then_inc(tile_ready[n % 2], 1)
                    elif kind == "kT":
                        pe.wait_ge(kt_ready, x + 1)
                        if x:
                            pe.wait_ge(tails_ready, 1)
                        for h in range(GH):
                            b = empty(("kT", x, h))
                            for c in range(NC):
                                ins = tr(ps[:, b, c * P:c * P + P], Kl[:, h, c * P:c * P + P], ident[:, :])
                            ins.then_inc(bank_ready[b], 1)
                        b = empty(("kTs", x))
                        for h in range(GH):
                            ins = tr(ps[0:TS, b, h * P:h * P + P], Kl[:, h, TP:T], ident[:, :])
                        ins.then_inc(bank_ready[b], 1)
                    elif kind == "sc":
                        pe.wait_ge(lev_ready, 2 * (LEV * x[0] + x[1] + 1))
                        hs = 64 >> x[1]
                        for h in range(GH):
                            b = empty(("sc", x, h))
                            for c in range(NC):
                                ins = mm(ps[:, b, 64 * c:64 * c + 64], Kl[:, h, c * P:c * P + P], Ql[:, h, 64 * c:64 * c + 64],
                                         start=True, stop=True)
                            if hs <= 2:
                                ins = mm(ps[0:TS, b, 256:272], Kl[:, h, TP:T], Ql[:, h, 256:272], start=True, stop=True)
                            ins.then_inc(bank_ready[b], 1)
                    elif kind == "diag":
                        for h in range(GH):
                            b = empty(("diag", x, h))
                            for c in range(NC):
                                ins = mm(ps[:, b, P * c:P * c + P], X[:, h, c * P:c * P + P], Q[:, h, c * P:c * P + P],
                                         start=True, stop=True)
                            ins.then_inc(bank_ready[b], 1)
                        b = empty(("diags", x))
                        for h in range(GH):
                            ins = mm(ps[0:TS, b, h * TS:h * TS + TS], X[:, h, TP:T], Q[:, h, TP:T], start=True, stop=True)
                        ins.then_inc(bank_ready[b], 1)
                    elif kind == "stA":
                        g, h = x // 4, x % 4
                        if h == 0:
                            after_banks(pe, [("kT", g, i) for i in range(GH)] + [("kTs", g)])
                            for t in range(NT):
                                after_tile(pe, "v", (g, t))
                        b = empty(("inc", x))
                        for c in range(NC):
                            ins = mm(ps[:, b, c * P:c * P + P], ktT[:, h, c, :], V[:, c, h * P:h * P + P], start=True, stop=True)
                        ins.then_inc(bank_ready[b], 1)
                    elif kind == "stB":
                        g, h, s = x // 4, x % 4, x % 2
                        if h == 0:
                            after_banks(pe, [("diag", g, i) for i in range(GH)] + [("diags", g)])
                        after_banks(pe, [("inc", x)])
                        pe.wait_ge(vb_ready, x + 1)
                        b = empty(("o", x))
                        hv = slice(h * P, h * P + P)
                        for c in range(NC):
                            cc = slice(c * P, c * P + P)
                            ins = mm(ps[:, b, cc], V[:, c, hv], A[:, h, cc], start=True, stop=(c == 0))
                            if c:
                                ins = mm(ps[:, b, cc], S[:, c - 1, :], qc[:, h, cc], start=False, stop=True)
                        ins.then_inc(bank_ready[b], 1)
                        b = empty(("os", x))
                        pe.wait_ge(s0_loaded[s], 16 * (x // 2 + 1))
                        mm(ps[:, b, 0:TS], V[0:TS, 4, hv], A[0:TS, h, TP:T], start=True, stop=False)
                        for r in range(NB):
                            ins = mm(ps[:, b, r * TB:r * TB + TB], S0[:, s, r, :], qc[:, h, TP + r * TB:TP + r * TB + TB],
                                     start=False, stop=(r == NB - 1))
                        ins.then_inc(bank_ready[b], 1)
                        for i in range(2):
                            b = empty(("si", x, i))
                            mm(ps[:, b, :], ktTs[0:TS, h, :], Vb[0:TS, 4 * i:4 * i + 4, :].rearrange("p b d -> p (b d)"),
                               start=True, stop=True).then_inc(bank_ready[b], 1)
                    elif kind == "stat":
                        from_dve()
                        for s in range(2):
                            ins = mm(ps[:, b + s, 0:HF], ones[:, :], (SG if x < 4 else squares1)[:, x % 2, s * HF:s * HF + HF], start=True, stop=True)
                        ins.then_inc(tile_ready[n % 2], 1)
                    elif kind == "pT":
                        r, b = TOK[x], 4 + x % 4
                        if x == 0:
                            pe.wait_ge(p_loaded, 48)
                            after_banks(pe, [("inc", 7), ("o", 7), ("os", 7), ("si", 7, 0), ("si", 7, 1)])
                        if x == 4:
                            pe.wait_ge(pt_copied, 1)
                        for k in range(2):
                            ins = tr(ps[:, b, k * P:k * P + r], pt[0:r, x, k * P:k * P + P], ident[0:r, 0:r])
                        ins.then_inc(pt_ready, 1)
                    elif kind == "pp":
                        pe.wait_ge(pt_copied, NT)
                        ple_proj(pe, x, 4 + 2 * x)
                    elif kind == "cvout":
                        from_dve()
                        after_banks(pe, [("si", 3, 0), ("os", 3)])
                        for k in range(KT):
                            ins = tr(ps[0:18, 6 + k // 4, (k % 4) * P:(k % 4) * P + P], ul[:, k, :], ident[:, :])
                        ins.then_inc(rows_ready, 1)

        x1_ready, r_ready, h2_ready = sem("x1_ready"), sem("rstd_ready"), sem("h2_ready")
        h2_out = [sem(f"h2_out{i}") for i in range(2)]
        wo_ready, h2t_ready, h2t_copied, lg_ready = sem("wo_ready"), sem("h2t_ready"), sem("h2t_copied"), sem("logits_ready")
        exp_asked, exp_done, m_ready, rank_ready = sem("exp_asked"), sem("exp_done"), sem("chosen_ready"), sem("rank_ready")
        rec_ready, rec_out, tab_in = sem("rec_ready"), sem("rec_out"), sem("table_loaded")
        step2 = {k: sem(f"{k}_step2") for k in ("act", "dve")}
        gu_loaded = [sem(f"gate_up_loaded{i}") for i in range(2)]
        dn_loaded = [sem(f"down_loaded{i}") for i in range(2)]
        xg_zero = sem("token_rows_zeroed")

        def load_expert(sp, e, s):
            gate = a["w_gate"][0][bass.ds(e, 1)].rearrange("e (k p) n -> p (e k) n", p=P)
            up = a["w_up"][0][bass.ds(e, 1)].rearrange("e (k p) n -> p (e k) n", p=P)
            sp.dma_start(wgu[s][:, :, 0:DE], gate).then_inc(gu_loaded[s], 16)
            sp.dma_start(wgu[s][:, :, DE:2 * DE], up).then_inc(gu_loaded[s], 16)

        def load_down(sp, e, s):
            down = a["w_down"][0][bass.ds(e, 1)].rearrange("e (k p) n -> p (e k) n", p=P)
            sp.dma_start(wdn[s][:, :, :], down).then_inc(dn_loaded[s], 16)

        with nc.Block() as block:

            @block.sync
            def _(sp):
                for s in range(2):
                    load_expert(sp, s, s)
                    load_down(sp, s, s)
                sp.dma_start(gfin, a["g_final"].unsqueeze(0).to_broadcast([P, D])).then_inc(gf_loaded, 16)
                for t in range(NT):
                    if t == NT - 1:
                        sp.wait_ge(wo_ready, NT)
                    for c in range(2) if t == NT - 1 else ():
                        sp.dma_start(W[:, (wo_chunk + c) % 2], a["w_ple_gate"][0][:, 512 * c:512 * c + 512].rearrange("(k p) n -> p k n", p=P)).then_inc(ple_w, 16)
                    sp.wait_ge(h2_ready, t + 1)
                    sp.dma_start(h2_dram[tok(t), :], h2[t % 2][0:TOK[t], :]).then_inc(h2_out[t % 2], 16)
                sp.wait_ge(rec_out, 16 * 2 * NT)
                sp.dma_start(tb[0:CAP], tab_dram.rearrange("(e r) c -> r e c", r=RANKS)[0:CAP]).then_inc(tab_in, 16)
                sp.wait_ge(h2_out[0], 48)
                sp.wait_ge(h2_out[1], 32)
                sp.wait_ge(tab_in, 16)
                sp.wait_ge(tab_set, 16)
                sp.wait_ge(gf_loaded, 16)

            @block.gpsimd
            def _(pool):
                for i in range(2):
                    nc.gpsimd.memset(xg[i], 0.0).then_inc(xg_zero, 1)
                    nc.gpsimd.memset(hid[i], 0.0).then_inc(xg_zero, 1)
                pool.wait_ge(xg_zero, 4)
                pool.wait_ge(tab_set, 16)
                for t in range(NT):
                    pool.wait_ge(rec_ready, t + 1)
                    for k in range(2):
                        n = TOK[t]
                        nc.gpsimd.indirect_dma_start(
                            out=tab_dram, out_offset=bass.IndirectOffsetOnAxis(ap=slot[0:n, t, k:k + 1], axis=0),
                            in_=rec[0:n, t, k, :], in_offset=None).then_inc(rec_out, 16)
                pool.wait_ge(rec_out, 16 * 2 * NT)

            @block.tensor
            def _(pe):
                mm, tr = nc.tensor.matmul, nc.tensor.transpose
                c0, c1 = wo_chunk, wo_chunk + 1

                def project(t, cols):
                    n, b = TOK[t], 2 * (t % 2)
                    if t >= 2:
                        pe.wait_ge(x1_ready, t - 1)
                    for k in range(KT):
                        for s in cols:
                            ins = mm(ps[at_half(t, s), b + s, :], m[:, k, tok(t)], W[:, (c0 + s) % 2, k, :], start=(k == 0), stop=(k == KT - 1))
                    if 1 in cols:
                        ins.then_inc(wo_ready, 1)

                def route(t):
                    n = TOK[t]
                    pe.wait_ge(h2_ready, t + 1)
                    if t:
                        pe.wait_ge(h2t_copied, t)
                    else:
                        pe.wait_ge(pp_copied, 2)
                    for k in range(KT):
                        ins = tr(ps[:, 4 + k // 4, (k % 4) * P:(k % 4) * P + n], h2[t % 2][0:n, k * P:k * P + P], ident[0:n, 0:n])
                    ins.then_inc(h2t_ready, 1)
                    pe.wait_ge(h2t_copied, t + 1)
                    if t:
                        pe.wait_ge(exp_asked, t)
                    else:
                        pe.wait_ge(r_loaded, 6 * 16)
                    for k in range(KT):
                        ins = mm(ps[0:n, 6, 0:36], h2T[:, k, 0:n], wr[:, k, :], start=(k == 0), stop=(k == KT - 1))
                    ins.then_inc(lg_ready, 1)

                def rank(t):
                    n = TOK[t]
                    pe.wait_ge(m_ready, t + 1)
                    for u in range(t):
                        mm(ps[0:n, 7, 0:NE], ones[:, 0:n], M[:, u, :], start=(u == 0), stop=False)
                    mm(ps[0:n, 7, 0:NE], tri[0:n, 0:n], M[0:n, t, :], start=(t == 0), stop=True).then_inc(rank_ready, 1)

                for s, c in enumerate((c0, c1)):
                    pe.wait_ge(w_loaded[c % 2], 16 * (c // 2 + 1))
                    for t in range(2):
                        project(t, (s,))
                route(0)
                for t in range(NT):
                    if 0 < t < NT - 2:
                        project(t + 1, (1,))
                        rank(t)
                    if t + 2 < NT:
                        project(t + 2, (0,) if t + 2 < NT - 1 else (0, 1))
                    if t == 3:
                        pe.wait_ge(x1_ready, 4)
                        ple_proj(pe, 2, 2)
                        rank(t)
                    if t == 4:
                        pe.wait_ge(x1_ready, 5)
                        ple_proj(pe, 3, 0)
                    if t in (0, NT - 1):
                        rank(t)
                    if t + 1 < NT:
                        route(t + 1)
                for u in range(NT):
                    ins = mm(ps[:, 5, 0:NE], ones[0:TOK[u], :], M[0:TOK[u], u, :], start=(u == 0), stop=(u == NT - 1))
                ins.then_inc(rank_ready, 1)
                pe.wait_ge(pp_copied, 3)
                ple_proj(pe, 4, 2)

            @block.scalar
            def _(act):
                step = Count()

                def link(ins):
                    ins.then_inc(step2["act"], 1)
                    act.wait_ge(step2["act"], step.next())

                def norm(t):
                    n = TOK[t]
                    act.wait_ge(x1_ready, t + 1)
                    if t >= 2:
                        act.wait_ge(h2_out[t % 2], 16 * (t // 2))
                        act.wait_ge(h2t_ready, t - 1)
                    nc.scalar.activation(h2[t % 2][0:n, :], x1[0:n, t, :], ACT.Square, accum_out=ss[0:n, t:t + 1]).then_inc(r_ready, 1)

                def turned(t):
                    n = TOK[t]
                    act.wait_ge(h2t_ready, t + 1)
                    if t:
                        act.wait_ge(lg_ready, t)
                    nc.scalar.activation(h2T[:, :, 0:n], ps[:, 4:6, :].rearrange("p s (k t) -> p (s k) t", k=4)[:, :, 0:n],
                                         ACT.Copy).then_inc(h2t_copied, 1)

                def keep_ple(t, b):
                    act.wait_ge(pp_ready, t + 1)
                    for c in range(2):
                        ins = nc.scalar.activation(ppr[t][0:TOK[t], 512 * c:512 * c + 512], ps[at_half(t, c), b + c, :], ACT.Copy)
                        if c == 0:
                            link(ins)
                    ins.then_inc(pp_copied, 1)

                keep_ple(0, 4)
                keep_ple(1, 6)
                norm(0)
                norm(1)
                turned(0)
                for t in range(NT):
                    n = TOK[t]
                    act.wait_ge(exp_asked, t + 1)
                    link(nc.scalar.activation(expj[0:n, :], lg[0:n, 0:4], ACT.Exp, bias=rf[0:n, 2:3], accum_out=rf[0:n, 0:1]))
                    nc.scalar.activation(rf[0:n, 1:2], top[0:n, 1, 1:2], ACT.Exp, bias=rf[0:n, 3:4]).then_inc(exp_done, 1)
                    if 0 < t < NT - 2:
                        norm(t + 1)
                    if t == NT - 3:
                        norm(NT - 1)
                    if t == 3:
                        keep_ple(2, 2)
                    if t + 1 < NT:
                        turned(t + 1)
                keep_ple(3, 0)
                keep_ple(4, 2)

            @block.vector
            def _(dve):
                v = nc.vector
                step = Count()

                def link(ins):
                    ins.then_inc(step2["dve"], 1)
                    dve.wait_ge(step2["dve"], step.next())

                dve.wait_ge(x1_loaded, NT * 16)
                dve.wait_ge(r_loaded, 6 * 16)
                link(v.memset(rec, 0))
                for k in range(2):
                    link(v.tensor_copy(rec[:, :, k, 0], tokno))
                    link(v.tensor_scalar(rec[:, :, k, 1], tokno, float(k * T), None, ALU.add))
                link(v.memset(g8, -3.0e38))

                def residual(t):
                    n, b = TOK[t], 2 * (t % 2)
                    dve.wait_ge(wo_ready, t + 1)
                    y = x1[0:n, t, :].rearrange("p (s d) -> p s d", s=2)
                    if n <= UP:
                        link(v.tensor_copy(moved[0:n], ps[at_half(t, 1), b + 1, :]))
                        link(v.tensor_tensor(y[:, 0], y[:, 0], ps[0:n, b, :], ALU.add))
                        v.tensor_tensor(y[:, 1], y[:, 1], moved[0:n], ALU.add).then_inc(x1_ready, 1)
                    else:
                        v.tensor_tensor(y, y, ps[0:n, b:b + 2, :], ALU.add).then_inc(x1_ready, 1)

                def scaled(t):
                    n = TOK[t]
                    dve.wait_ge(r_ready, t + 1)
                    rstd(v, link, ss[0:n, t:t + 1], rs[0:n, t:t + 1])
                    v.scalar_tensor_tensor(h2[t % 2][0:n, :], x1[0:n, t, :], rs[0:n, t:t + 1], gffn[0:n, :], ALU.mult,
                                           ALU.mult).then_inc(h2_ready, 1)

                def choose(t):
                    n = TOK[t]
                    dve.wait_ge(lg_ready, t + 1)
                    L = lg[0:n, :]
                    link(v.tensor_tensor(L, ps[0:n, 6, 0:36], rb[0:n, :], ALU.add))
                    link(v.tensor_copy(g8[0:n, 0:4], L[:, 0:4]))
                    link(v.max(top[0:n, 0, :], g8[0:n, :]))
                    link(v.max_index(topi[0:n, 0, :], top[0:n, 0, :], g8[0:n, :]))
                    link(v.tensor_scalar(rf[0:n, 2:3], top[0:n, 0, 0:1], -1.0, None, ALU.mult))
                    link(v.tensor_copy(rf[0:n, 4:5], topi[0:n, 0, 0:1]))
                    link(v.tensor_scalar(junk[0:n, 0:4], iota[0:n, 0:4], rf[0:n, 4:5], None, ALU.is_equal))
                    link(v.tensor_tensor(own[0:n], L[:, 4:36].rearrange("p (g e) -> p g e", g=NG),
                                         junk[0:n, 0:4].unsqueeze(2).to_broadcast([n, NG, EG]), ALU.mult))
                    link(v.tensor_reduce(sel[0:n, :], own[0:n].rearrange("p g e -> p e g"), AX.X, ALU.add))
                    link(v.max(top[0:n, 1, :], sel[0:n, :]))
                    link(v.max_index(topi[0:n, 1, :], top[0:n, 1, :], sel[0:n, :]))
                    v.tensor_scalar(rf[0:n, 3:4], top[0:n, 1, 0:1], -1.0, None, ALU.mult).then_inc(exp_asked, 1)
                    link(v.tensor_copy(rf[0:n, 5:7], topi[0:n, 1, 0:2]))
                    link(v.scalar_tensor_tensor(rf[0:n, 7:9], rf[0:n, 4:5].to_broadcast([n, 2]), float(EG), rf[0:n, 5:7],
                                                ALU.mult, ALU.add))
                    link(v.tensor_tensor(oh[0:n], iota[0:n, :].unsqueeze(1).to_broadcast([n, 2, NE]),
                                         rf[0:n, 7:9].unsqueeze(2).to_broadcast([n, 2, NE]), ALU.is_equal))
                    v.tensor_tensor(M[0:n, t, :], oh[0:n, 0, :], oh[0:n, 1, :], ALU.add).then_inc(m_ready, 1)

                def place(t):
                    n = TOK[t]
                    dve.wait_ge(exp_done, t + 1)
                    link(v.tensor_scalar(rf[0:n, 9:10], rf[0:n, 1:2], 1.0, rf[0:n, 0:1], ALU.add, ALU.mult))
                    link(v.reciprocal(rf[0:n, 11:12], rf[0:n, 9:10]))
                    link(v.tensor_tensor(rf[0:n, 12:13], rf[0:n, 11:12], rf[0:n, 1:2], ALU.mult))
                    dve.wait_ge(rank_ready, t + 1)
                    link(v.tensor_tensor(before[0:n], oh[0:n], ps[0:n, 7, 0:NE].unsqueeze(1).to_broadcast([n, 2, NE]), ALU.mult))
                    link(v.tensor_reduce(rf[0:n, 13:15], before[0:n], AX.X, ALU.add))
                    link(v.scalar_tensor_tensor(slot[0:n, t, :], rf[0:n, 7:9], float(RANKS), rf[0:n, 13:15], ALU.mult, ALU.add))
                    link(v.tensor_copy(rec[0:n, t, :, 2].bitcast(F32), rf[0:n, 11:13]))
                    v.engine_nop().then_inc(rec_ready, 1)

                for t in range(2):
                    residual(t)
                    scaled(t)
                for t in range(NT):
                    choose(t)
                    if 0 < t < NT - 2:
                        residual(t + 1)
                        scaled(t + 1)
                    place(t)
                    if t == NT - 3:
                        residual(NT - 1)
                        scaled(NT - 1)
                dve.wait_ge(rank_ready, NT + 1)
                link(v.tensor_reduce(rf[:, 15:16], ps[:, 5, 0:NE], AX.X, ALU.max))
                link(v.tensor_scalar(flag, rf[0:1, 15:16], float(CAP), None, ALU.is_gt))

        gathered = [sem(f"gathered{i}") for i in range(2)]
        g_idx, s_idx = sem("gather_index"), sem("scatter_index")
        t_ready, t_cp_a, t_cp_v = sem("xg_transposed"), sem("xgT_copied_act"), sem("xgT_copied_dve")
        gu_ready, tanh_done, hid_ready = sem("gate_up_ready"), sem("tanh_done"), sem("hid_ready")
        up_copied = sem("up_copied")
        ht_ready, ht_copied, dn_ready = sem("hidT_ready"), sem("hidT_copied"), sem("down_ready")
        yo_a, yo_v = sem("rows_copied_act"), sem("rows_copied_dve")
        y_out = [sem(f"expert_rows_out{i}") for i in range(2)]
        vstep = sem("expert_dve_step")

        with nc.Block() as block:

            @block.sync
            def _(sp):
                sp.wait_ge(gu_ready, 1)
                load_expert(sp, 2, 0)
                with sp.Fori(0, NE // 2 - 2) as i:
                    for s in range(2):
                        e = 2 * i + s + 1
                        sp.wait_ge(gu_ready, e + 1)
                        load_expert(sp, e + 2, 1 - s)
                        sp.wait_ge(dn_ready, e)
                        load_down(sp, e + 1, s)
                sp.wait_ge(gu_ready, NE - 2)
                load_expert(sp, NE - 1, 1)
                for e in (NE - 3, NE - 2):
                    sp.wait_ge(dn_ready, e)
                    load_down(sp, e + 1, (e + 1) % 2)
                sp.wait_ge(ple_w, 32)

            @block.gpsimd
            def _(pool):
                zero, bound = pool.to_reg(0), pool.alloc_register("bound")

                def gather(e, s, first=False):
                    if not first:
                        pool.wait_ge(t_ready, e - 1)
                    nc.gpsimd.tensor_copy(gidx[s][0:CAP], tb[0:CAP, bass.ds(e, 1), 0]).then_inc(g_idx, 1)
                    pool.wait_ge(g_idx, e + 1)
                    pool.reg_add(bound, zero, T - 1)
                    nc.gpsimd.indirect_dma_start(out=xg[s][0:CAP], out_offset=None, in_=h2_dram,
                                                 in_offset=bass.IndirectOffsetOnAxis(ap=gidx[s][0:CAP], axis=0),
                                                 bounds_check=bound, oob_is_err=False).then_inc(gathered[s], 16)

                def scatter(e, s):
                    pool.wait_ge(yo_a, e + 1)
                    pool.wait_ge(yo_v, e + 1)
                    nc.gpsimd.tensor_copy(sidx[s][0:CAP], tb[0:CAP, bass.ds(e, 1), 1]).then_inc(s_idx, 1)
                    pool.wait_ge(s_idx, e + 1)
                    pool.reg_add(bound, zero, 2 * T - 1)
                    nc.gpsimd.indirect_dma_start(out=y_dram, out_offset=bass.IndirectOffsetOnAxis(ap=sidx[s][0:CAP], axis=0),
                                                 in_=yo[s][0:CAP], in_offset=None,
                                                 bounds_check=bound, oob_is_err=False).then_inc(y_out[s], 16)

                gather(0, 0, True)
                gather(1, 1, True)
                gather(2, 0)
                with pool.Fori(0, NE // 2 - 2) as i:
                    for s in range(2):
                        gather(2 * i + s + 3, 1 - s)
                        scatter(2 * i + s, s)
                gather(NE - 1, 1)
                for e in range(NE - 4, NE):
                    scatter(e, e % 2)
                for s in range(2):
                    pool.wait_ge(y_out[s], 16 * (NE // 2))

            def wait_for(eng, sem, value):
                if not isinstance(value, int) or value > 0:
                    eng.wait_ge(sem, value)

            def phases(eng, prologue, body):
                prologue()
                for s in range(2):
                    body(s, s, True, True)
                with eng.Fori(1, NE // 2 - 1) as i:
                    for s in range(2):
                        body(2 * i + s, s, True, True)
                body(NE - 2, 0, True, False)
                body(NE - 1, 1, False, False)

            @block.tensor
            def _(pe):
                mm, tr = nc.tensor.matmul, nc.tensor.transpose

                def turn(e, s, n):
                    pe.wait_ge(gathered[s], n)
                    wait_for(pe, t_cp_a, e)
                    wait_for(pe, t_cp_v, e)
                    for k in range(KT):
                        r = CAP if k else P
                        ins = tr(ps[:, k // 4, (k % 4) * P:(k % 4) * P + r], xg[s][0:r, k * P:k * P + P], ident[0:r, 0:r])
                    ins.then_inc(t_ready, 1)

                def gate_up(e, s, n):
                    pe.wait_ge(gu_loaded[s], n)
                    pe.wait_ge(t_cp_a, e + 1)
                    pe.wait_ge(t_cp_v, e + 1)
                    wait_for(pe, hid_ready, e - 1)
                    for k in range(KT):
                        for u in range(2):
                            ins = mm(ps[u * UP:u * UP + CAP, 2 + s, 0:DE], xgT[s][:, k, 0:CAP], wgu[s][:, k, u * DE:u * DE + DE],
                                     start=(k == 0), stop=(k == KT - 1))
                    ins.then_inc(gu_ready, 1)

                def body(e, s, more, more2):
                    half = (e - s) // 2 if isinstance(e, int) else None
                    i16 = lambda add: 16 * (half + add) if half is not None else 8 * (e - s) + 16 * add
                    pe.wait_ge(hid_ready, e + 1)
                    for k in range(2):
                        r = CAP if k else P
                        ins = tr(ps[:, 6, k * P:k * P + r], hid[s][0:r, k * P:k * P + P], ident[0:r, 0:r])
                    ins.then_inc(ht_ready, 1)
                    if more:
                        n1 = 1 if s == 0 else 2
                        gate_up(e + 1, 1 - s, 2 * i16(n1))
                    if more2:
                        turn(e + 2, s, i16(2))
                    pe.wait_ge(dn_loaded[s], i16(1))
                    pe.wait_ge(ht_copied, e + 1)
                    wait_for(pe, yo_a, e)
                    wait_for(pe, yo_v, e)
                    for k in range(2):
                        for c in range(2):
                            ins = mm(ps[c * UP:c * UP + CAP, 4 + c, :], hidT[s][:, k, 0:CAP], wdn[s][:, k, 512 * c:512 * c + 512], start=(k == 0),
                                     stop=(k == 1))
                    ins.then_inc(dn_ready, 1)

                def prologue():
                    turn(0, 0, 16)
                    turn(1, 1, 16)
                    gate_up(0, 0, 32)

                phases(pe, prologue, body)

            @block.scalar
            def _(act):
                def copy_t(e, s):
                    act.wait_ge(t_ready, e + 1)
                    wait_for(act, gu_ready, e - 1)
                    nc.scalar.activation(xgT[s][:, 0:4, 0:CAP], ps[:, 0, :].rearrange("p (k t) -> p k t", k=4)[:, :, 0:CAP],
                                         ACT.Copy).then_inc(t_cp_a, 1)

                def gate(e, s):
                    act.wait_ge(gu_ready, e + 1)
                    wait_for(act, hid_ready, e - 1)
                    nc.scalar.activation(sg[s][0:CAP], ps[0:CAP, 2 + s, 0:DE], ACT.Tanh, scale=0.5).then_inc(tanh_done, 1)
                    nc.scalar.activation(up[s][0:CAP], ps[UP:UP + CAP, 2 + s, 0:DE], ACT.Copy).then_inc(up_copied, 1)

                def rows_out(e, s, n):
                    act.wait_ge(dn_ready, e + 1)
                    wait_for(act, y_out[s], n)
                    nc.scalar.activation(yo[s][0:CAP, 0:512], ps[0:CAP, 4, :], ACT.Copy).then_inc(yo_a, 1)

                def body(e, s, more, more2):
                    if more:
                        gate(e + 1, 1 - s)
                    if more2:
                        copy_t(e + 2, s)
                    rows_out(e, s, 8 * (e - s))

                def prologue():
                    copy_t(0, 0)
                    copy_t(1, 1)
                    gate(0, 0)

                phases(act, prologue, body)

            @block.vector
            def _(dve):
                v = nc.vector

                def copy_t(e, s):
                    dve.wait_ge(t_ready, e + 1)
                    wait_for(dve, gu_ready, e - 1)
                    v.tensor_copy(xgT[s][:, 4:8, 0:CAP], ps[:, 1, :].rearrange("p (k t) -> p k t", k=4)[:, :, 0:CAP]).then_inc(t_cp_v, 1)

                def gate(e, s):
                    dve.wait_ge(tanh_done, e + 1)
                    v.tensor_scalar(sg[s][0:CAP], sg[s][0:CAP], 0.5, 0.5, ALU.mult, ALU.add).then_inc(vstep, 1)
                    dve.wait_ge(vstep, 2 * e + 1)
                    v.tensor_tensor(sg[s][0:CAP], sg[s][0:CAP], ps[0:CAP, 2 + s, 0:DE], ALU.mult).then_inc(vstep, 1)
                    dve.wait_ge(vstep, 2 * e + 2)
                    dve.wait_ge(up_copied, e + 1)
                    wait_for(dve, ht_ready, e - 1)
                    v.scalar_tensor_tensor(hid[s][0:CAP], sg[s][0:CAP], tb[0:CAP, bass.ds(e, 1), 2].bitcast(F32),
                                           up[s][0:CAP], ALU.mult, ALU.mult).then_inc(hid_ready, 1)

                def rows_out(e, s, n):
                    dve.wait_ge(dn_ready, e + 1)
                    wait_for(dve, y_out[s], n)
                    v.tensor_copy(yo[s][0:CAP, 512:1024], ps[UP:UP + CAP, 5, :]).then_inc(yo_v, 1)

                def body(e, s, more, more2):
                    dve.wait_ge(ht_ready, e + 1)
                    wait_for(dve, dn_ready, e - 1)
                    v.tensor_copy(hidT[s][:, :, 0:CAP], ps[:, 6, 0:DE].rearrange("p (k t) -> p k t", k=2)[:, :, 0:CAP]).then_inc(ht_copied, 1)
                    if more:
                        gate(e + 1, 1 - s)
                    if more2:
                        copy_t(e + 2, s)
                    rows_out(e, s, 8 * (e - s))

                def prologue():
                    copy_t(0, 0)
                    copy_t(1, 1)
                    gate(0, 0)

                phases(dve, prologue, body)

        over = nc.values_load(flag, min_val=0, max_val=1)
        f_w, f_tab, f_xg, f_y = (sem(n) for n in ("more_weights", "more_table", "more_gathered", "more_stored"))
        f_t, f_tc, f_gu, f_tanh, f_hid, f_ht, f_hc, f_dn, f_yo, f_v = (sem("more_" + n) for n in (
            "transposed", "copied", "gate_up", "tanh", "hid", "hidT", "hidT_copied", "down", "rows", "dve_step"))
        BLOCKS = (T - CAP + P - 1) // P

        with nc.If(over > 0):
            with nc.Block() as block:

                @block.sync
                def _(sp):
                    def blocks(e):
                        for b in range(BLOCKS):
                            if not (isinstance(e, int) and b == 0):
                                sp.wait_ge(f_y, 16 * BLOCKS * e + 16 * b)
                            if b == 0:
                                one = bass.ds(e, 1)
                                sp.dma_start(wgu[0][:, :, 0:DE], a["w_gate"][0][one].rearrange("e (k p) n -> p (e k) n", p=P)).then_inc(f_w, 16)
                                sp.dma_start(wgu[0][:, :, DE:2 * DE], a["w_up"][0][one].rearrange("e (k p) n -> p (e k) n", p=P)).then_inc(f_w, 16)
                                sp.dma_start(wdn[0], a["w_down"][0][one].rearrange("e (k p) n -> p (e k) n", p=P)).then_inc(f_w, 16)
                                sp.wait_ge(f_w, 48 * e + 48)
                            sp.dma_start(ftab, tab_dram[bass.ds(RANKS * e + P * b + CAP, P), :]).then_inc(f_tab, 16)

                    blocks(0)
                    with sp.Fori(1, NE) as e:
                        blocks(e)
                    sp.wait_ge(f_y, 16 * BLOCKS * NE)

                @block.gpsimd
                def _(pool):
                    zero, bound = pool.to_reg(0), pool.alloc_register("more_bound")
                    with pool.Fori(0, NE * BLOCKS) as j:
                        pool.wait_ge(f_tab, 16 * j + 16)
                        pool.reg_add(bound, zero, T - 1)
                        nc.gpsimd.indirect_dma_start(out=xg[0], out_offset=None, in_=h2_dram,
                                                     in_offset=bass.IndirectOffsetOnAxis(ap=ftab[:, 0:1], axis=0),
                                                     bounds_check=bound, oob_is_err=False).then_inc(f_xg, 16)
                        pool.wait_ge(f_yo, j + 1)
                        pool.reg_add(bound, zero, 2 * T - 1)
                        nc.gpsimd.indirect_dma_start(out=y_dram, out_offset=bass.IndirectOffsetOnAxis(ap=ftab[:, 1:2], axis=0),
                                                     in_=yo[0], in_offset=None, bounds_check=bound,
                                                     oob_is_err=False).then_inc(f_y, 16)

                @block.tensor
                def _(pe):
                    mm, tr = nc.tensor.matmul, nc.tensor.transpose
                    with pe.Fori(0, NE * BLOCKS) as j:
                        pe.wait_ge(f_xg, 16 * j + 16)
                        for k in range(KT):
                            ins = tr(ps[:, k // 4, (k % 4) * P:(k % 4) * P + P], xg[0][:, k * P:k * P + P], ident[:, :])
                        ins.then_inc(f_t, 1)
                        pe.wait_ge(f_tc, j + 1)
                        for k in range(KT):
                            ins = mm(ps[:, 2, :], xgT[0][:, k, :], wgu[0][:, k, :], start=(k == 0), stop=(k == KT - 1))
                        ins.then_inc(f_gu, 1)
                        pe.wait_ge(f_hid, j + 1)
                        for k in range(2):
                            ins = tr(ps[:, 6, k * P:k * P + P], hid[0][:, k * P:k * P + P], ident[:, :])
                        ins.then_inc(f_ht, 1)
                        pe.wait_ge(f_hc, j + 1)
                        for k in range(2):
                            for c in range(2):
                                ins = mm(ps[:, 4 + c, :], hidT[0][:, k, :], wdn[0][:, k, 512 * c:512 * c + 512],
                                         start=(k == 0), stop=(k == 1))
                        ins.then_inc(f_dn, 1)

                @block.scalar
                def _(act):
                    with act.Fori(0, NE * BLOCKS) as j:
                        act.wait_ge(f_gu, j + 1)
                        nc.scalar.activation(sg[0], ps[:, 2, 0:DE], ACT.Tanh, scale=0.5).then_inc(f_tanh, 1)

                @block.vector
                def _(dve):
                    v = nc.vector
                    with dve.Fori(0, NE * BLOCKS) as j:
                        dve.wait_ge(f_t, j + 1)
                        v.tensor_copy(xgT[0], ps[:, 0:2, :].rearrange("p s (k t) -> p (s k) t", k=4)).then_inc(f_tc, 1)
                        dve.wait_ge(f_tanh, j + 1)
                        v.tensor_scalar(sg[0], sg[0], 0.5, 0.5, ALU.mult, ALU.add).then_inc(f_v, 1)
                        dve.wait_ge(f_v, 2 * j + 1)
                        v.tensor_tensor(sg[0], sg[0], ps[:, 2, 0:DE], ALU.mult).then_inc(f_v, 1)
                        dve.wait_ge(f_v, 2 * j + 2)
                        v.scalar_tensor_tensor(hid[0], sg[0], ftab[:, 2:3].bitcast(F32), ps[:, 2, DE:2 * DE], ALU.mult,
                                               ALU.mult).then_inc(f_hid, 1)
                        dve.wait_ge(f_ht, j + 1)
                        v.tensor_copy(hidT[0], ps[:, 6, 0:DE].rearrange("p (k t) -> p k t", k=2)).then_inc(f_hc, 1)
                        dve.wait_ge(f_dn, j + 1)
                        v.tensor_copy(yo[0].rearrange("p (s d) -> p s d", s=2), ps[:, 4:6, :]).then_inc(f_yo, 1)

        y_in = [sem(f"expert_rows_in{t}") for t in range(NT)]
        x2_ready, r3_ready, scale_ready, h3t_ready, h3t_copied = (sem(n) for n in (
            "x2_ready", "squares3_ready", "scale3_ready", "x2t_ready", "x2t_copied"))
        pg_ready, tanh3, x3_ready, r4_ready, out_ready = (sem(n) for n in (
            "ple_gate_ready", "tanh3_done", "x3_ready", "rstd4_ready", "out_ready"))
        y_stored = [sem(f"y_stored{i}") for i in range(2)]
        step3 = {k: sem(f"{k}_step3") for k in ("act", "dve")}

        with nc.Block() as block:

            @block.sync
            def _(sp):
                for t in range(NT):
                    for k in range(2):
                        r0 = k * T + t * P
                        sp.dma_start(yk[t][k][0:TOK[t], :], y_dram[r0:r0 + TOK[t], :]).then_inc(y_in[t], 16)
                for t in range(NT):
                    n = TOK[t]
                    sp.wait_ge(out_ready, t + 1)
                    dst = o["y_prompt"][0, t * P:t * P + P, :] if t < 4 else o["y_sample"].rearrange("b t d -> (b t) d")
                    sp.dma_start(dst, out3[t % 2][0:n, :]).then_inc(y_stored[t % 2], 16)
                sp.wait_ge(y_stored[0], 16 * 3)
                sp.wait_ge(y_stored[1], 16 * 2)

            @block.tensor
            def _(pe):
                mm, tr = nc.tensor.matmul, nc.tensor.transpose
                def turn(t):
                    n = TOK[t]
                    pe.wait_ge(x2_ready, t + 1)
                    if t:
                        pe.wait_ge(h3t_copied, t)
                    for k in range(KT):
                        ins = tr(ps[:, k // 4, (k % 4) * P:(k % 4) * P + n], x1[0:n, t, k * P:k * P + P], ident[0:n, 0:n])
                    ins.then_inc(h3t_ready, 1)

                turn(0)
                for t in range(NT):
                    n, b = TOK[t], 2 + 2 * (t % 2)
                    if t >= 2:
                        pe.wait_ge(x3_ready, t - 1)
                    pe.wait_ge(h3t_copied, t + 1)
                    for k in range(KT):
                        for c in range(2):
                            ins = mm(ps[at_half(t, c), b + c, :], h3T[t % 2][:, k, 0:n], W[:, (wo_chunk + c) % 2, k, :], start=(k == 0), stop=(k == KT - 1))
                        if k == 0 and t == 0:
                            turn(1)
                    ins.then_inc(pg_ready, 1)
                    if t + 2 < NT:
                        turn(t + 2)

            @block.scalar
            def _(act):
                def rms(t, done):
                    n = TOK[t]
                    nc.scalar.activation(squares[0:n, :], x1[0:n, t, :], ACT.Square, accum_out=ss[0:n, t:t + 1]).then_inc(done, 1)
                    act.wait_ge(done, t + 1)

                def norm2(t):
                    act.wait_ge(x2_ready, t + 1)
                    rms(t, r3_ready)

                norm2(0)
                norm2(1)
                for t in range(NT):
                    n, b = TOK[t], 2 + 2 * (t % 2)
                    if t + 2 < NT:
                        norm2(t + 2)
                    act.wait_ge(pg_ready, t + 1)
                    act.wait_ge(scale_ready, t + 1)
                    if t >= 2:
                        act.wait_ge(x3_ready, t - 1)
                    for c in range(2):
                        nc.scalar.activation(s3[t % 2][0:n, 512 * c:512 * c + 512], ps[at_half(t, c), b + c, :], ACT.Tanh,
                                             scale=half_r[0:n, t:t + 1]).then_inc(tanh3, 1)
                    act.wait_ge(x3_ready, t + 1)
                    rms(t, r4_ready)

            @block.vector
            def _(dve):
                v = nc.vector
                step = Count()

                def link(ins):
                    ins.then_inc(step3["dve"], 1)
                    dve.wait_ge(step3["dve"], step.next())

                def experts_in(t):
                    n, x = TOK[t], x1[0:TOK[t], t, :]
                    dve.wait_ge(y_in[t], 32)
                    link(v.tensor_tensor(x, x, yk[t][0][0:n, :], ALU.add))
                    v.tensor_tensor(x, x, yk[t][1][0:n, :], ALU.add).then_inc(x2_ready, 1)

                def scale_of(t):
                    n = TOK[t]
                    dve.wait_ge(r3_ready, t + 1)
                    rstd(v, link, ss[0:n, t:t + 1], rs[0:n, t:t + 1])
                    v.tensor_scalar(half_r[0:n, t:t + 1], rs[0:n, t:t + 1], 0.5, None, ALU.mult).then_inc(scale_ready, 1)

                def turned(t):
                    n = TOK[t]
                    dve.wait_ge(h3t_ready, t + 1)
                    if t >= 2:
                        dve.wait_ge(pg_ready, t - 1)
                    v.tensor_tensor(h3T[t % 2][:, :, 0:n], ps[:, 0:2, :].rearrange("p s (k t) -> p (s k) t", k=4)[:, :, 0:n],
                                    gain[:, 16:24].unsqueeze(2).to_broadcast([P, 8, n]), ALU.mult).then_inc(h3t_copied, 1)

                for t in range(2):
                    experts_in(t)
                    turned(t)
                    scale_of(t)
                for t in range(NT):
                    n, x = TOK[t], x1[0:TOK[t], t, :]
                    if t + 2 < NT:
                        experts_in(t + 2)
                        scale_of(t + 2)
                    dve.wait_ge(tanh3, 2 * t + 2)
                    s = s3[t % 2][0:n, :]
                    link(v.scalar_tensor_tensor(s, s, 1.0, ppr[t][0:n, :], ALU.add, ALU.mult))
                    v.scalar_tensor_tensor(x, s, 0.5, x, ALU.mult, ALU.add).then_inc(x3_ready, 1)
                    if t + 2 < NT:
                        turned(t + 2)
                    dve.wait_ge(r4_ready, t + 1)
                    rstd(v, link, ss[0:n, t:t + 1], rs[0:n, t:t + 1])
                    if t >= 2:
                        dve.wait_ge(y_stored[t % 2], 16 * (t // 2))
                    v.scalar_tensor_tensor(out3[t % 2][0:n, :], x, rs[0:n, t:t + 1], gfin[0:n, :], ALU.mult, ALU.mult).then_inc(out_ready, 1)


_INS = ['x_prompt', 'x_sample', 'state_hgrn', 'state_conv', 'p_prompt', 'p_sample', 'g_mix', 'w_in', 'hg_lower',
        'g_hg_out', 'w_br_a', 'w_conv', 'w_br_b', 'w_out', 'g_ffn', 'w_router_group', 'b_router_group',
        'w_router_expert', 'b_router_expert', 'w_gate', 'w_up', 'w_down', 'g_ple', 'w_ple_gate', 'w_ple_proj',
        'g_final']
_OUTS = [("y_prompt", (1, TP, D)), ("y_sample", (NB, TB, D)), ("hgrn_prompt", (1, 1, NH, DK, DK)),
         ("conv_prompt", (1, 1, 2, D)), ("hgrn_sample", (1, NB, NH, DK, DK)), ("conv_sample", (1, NB, 2, D))]


def constants():
    s, t = np.arange(P)[:, None], np.arange(P)[None, :]
    lmask = np.zeros((P, LEV, 256), np.float32)
    smask = np.zeros((TS, 2, 16), np.float32)
    for l in range(LEV):
        hs = 64 >> l
        pair = (s // (2 * hs) == t // (2 * hs)) & (s % (2 * hs) < hs) & (t % (2 * hs) >= hs)
        late = pair[:, (np.arange(P) % (2 * hs)) >= hs]
        lmask[:, l] = np.tile(late, (1, NC))
        if hs <= 2:
            smask[:, l - 5] = late[0:TS, 0:16]
    small = np.zeros((P, 64), np.float32)
    small[:, 0:8] = (s // TB == np.arange(NB)[None, :])
    small[:, 8:40] = np.arange(NE)[None, :]
    small[:, 40:45] = s + P * np.arange(NT)[None, :]
    return dict(c_ident=np.eye(P, dtype=np.float32), c_tri=(s < t).astype(np.float32), c_lmask=lmask,
                c_smask=smask, c_small=small)


def kernel(**inputs):
    import concourse.bacc as _bacc
    from concourse.bass_utils import run_bass_kernel_spmd as _run

    nc = _bacc.Bacc("TRN2", target_bir_lowering=False, num_devices=1)
    arrays, ins, outs = {}, {}, {}
    for name in _INS:
        arrays[f"in_{name}"] = np.ascontiguousarray(inputs[name])
    for name, x in constants().items():
        arrays[f"in_{name}"] = x
    for name, x in arrays.items():
        ins[name[3:]] = nc.dram_tensor(name, x.shape, mybir.dt.from_np(x.dtype), kind="ExternalInput").ap()
    for name, shape in _OUTS:
        outs[name] = nc.dram_tensor(f"out_{name}", shape, F32, kind="ExternalOutput").ap()
    layer(nc, ins, outs)
    r = _run(nc, [arrays], core_ids=[0])
    return tuple(r.results[0][f"out_{name}"] for name, _ in _OUTS)
```
